# Optimizing a Trainium2 kernel written in Bass

```python
import jax, jax.numpy as jnp
from jax import lax
import numpy as np

D_MODEL = 1024
BATCH = 1
SEQ = 512
DEPTH = 2

CHUNK = 64
N_META = 16
WINDOW = 128
WINDOW_CHUNKS = WINDOW // CHUNK

HEAD_DIM = 64
ATTN_WIDTH = D_MODEL // 2
N_Q_HEADS = ATTN_WIDTH // HEAD_DIM
N_KV_HEADS = max(1, N_Q_HEADS // 4)
GQA_GROUP = N_Q_HEADS // N_KV_HEADS
KV_WIDTH = N_KV_HEADS * HEAD_DIM
ROPE_THETA = 10000.0

POOL_WIDTH = D_MODEL - ATTN_WIDTH
POOL_SIZES = (2, 4, 8, 16)
N_POOL_GROUPS = len(POOL_SIZES)
POOL_GROUP = POOL_WIDTH // N_POOL_GROUPS

IN_WIDTH = ATTN_WIDTH + 2 * KV_WIDTH + POOL_WIDTH
MIX_WIDTH = ATTN_WIDTH + POOL_WIDTH

D_FF = ((8 * D_MODEL // 3 + 127) // 128) * 128
CONV_WIDTH = 3

EPS = 1e-6
NEG_INF = -1e30

kernel_name = "hymba_swa_sink_pool_convffn"

def rms_norm(x, g):
    xf = x.astype(jnp.float32)
    y = xf * lax.rsqrt(jnp.mean(xf * xf, axis=-1, keepdims=True) + EPS)
    return (y * g.astype(jnp.float32)).astype(x.dtype)

def rope_tables(length):
    inv = 1.0 / (ROPE_THETA ** (jnp.arange(0, HEAD_DIM, 2, dtype=jnp.float32) / HEAD_DIM))
    ang = jnp.arange(length, dtype=jnp.float32)[:, None] * inv[None, :]
    return jnp.cos(ang), jnp.sin(ang)

def apply_rope(x, cos, sin):
    xf = x.astype(jnp.float32)
    x1, x2 = jnp.split(xf, 2, axis=-1)
    c = cos[None, :, None, :]
    s = sin[None, :, None, :]
    return jnp.concatenate([x1 * c - x2 * s, x2 * c + x1 * s], axis=-1).astype(x.dtype)

def sink_softmax(s, sink):
    sk = sink.astype(jnp.float32)[..., None]
    m = jnp.maximum(jnp.max(s, axis=-1, keepdims=True), sk)
    p = jnp.exp(s - m)
    return p / (jnp.sum(p, axis=-1, keepdims=True) + jnp.exp(sk - m))

def window_stack(t, n_chunks):
    tp = jnp.pad(t, ((0, 0), (WINDOW_CHUNKS - 1, 0), (0, 0), (0, 0), (0, 0)))
    return jnp.concatenate([tp[:, i:i + n_chunks] for i in range(WINDOW_CHUNKS)], axis=2)

def sliding_sink_attention(q, k, v, sinks):
    B, L = q.shape[:2]
    nc = (L - N_META) // CHUNK
    sk = sinks.reshape(N_KV_HEADS, GQA_GROUP)
    km, vm = k[:, :N_META], v[:, :N_META]

    qm = q[:, :N_META].reshape(B, N_META, N_KV_HEADS, GQA_GROUP, HEAD_DIM)
    s_m = jnp.einsum('bqkgd,bmkd->bqkgm', qm, km, preferred_element_type=jnp.float32)
    p_m = sink_softmax(s_m, sk).astype(v.dtype)
    o_m = jnp.einsum('bqkgm,bmkd->bqkgd', p_m, vm).reshape(B, N_META, N_Q_HEADS * HEAD_DIM)

    qr = q[:, N_META:].reshape(B, nc, CHUNK, N_KV_HEADS, GQA_GROUP, HEAD_DIM)
    kr = k[:, N_META:].reshape(B, nc, CHUNK, N_KV_HEADS, HEAD_DIM)
    vr = v[:, N_META:].reshape(B, nc, CHUNK, N_KV_HEADS, HEAD_DIM)
    kw = window_stack(kr, nc)
    vw = window_stack(vr, nc)
    s_meta = jnp.einsum('bcqkgd,bmkd->bcqkgm', qr, km, preferred_element_type=jnp.float32)
    s_win = jnp.einsum('bcqkgd,bcnkd->bcqkgn', qr, kw, preferred_element_type=jnp.float32)
    chunk_idx = jnp.arange(nc)[:, None]
    back = jnp.repeat(jnp.arange(WINDOW_CHUNKS - 1, -1, -1), CHUNK)[None, :]
    valid = (chunk_idx - back) >= 0
    s_win = jnp.where(valid[None, :, None, None, None, :], s_win, NEG_INF)
    p = sink_softmax(jnp.concatenate([s_meta, s_win], axis=-1), sk).astype(v.dtype)
    o_r = (jnp.einsum('bcqkgm,bmkd->bcqkgd', p[..., :N_META], vm)
           + jnp.einsum('bcqkgn,bcnkd->bcqkgd', p[..., N_META:], vw))
    o_r = o_r.reshape(B, nc * CHUNK, N_Q_HEADS * HEAD_DIM)
    return jnp.concatenate([o_m, o_r], axis=1)

def multiscale_pool(u, w_pool, scale):
    B, L = u.shape[:2]
    uf = u.astype(jnp.float32).reshape(B, L, N_POOL_GROUPS, POOL_GROUP)
    cs = jnp.cumsum(uf, axis=1)
    t = jnp.arange(L)
    outs = []
    for gi, w in enumerate(POOL_SIZES):
        c = cs[:, :, gi]
        prev = jnp.pad(c, ((0, 0), (w, 0), (0, 0)))[:, :L]
        cnt = jnp.minimum(t + 1, w).astype(jnp.float32)[None, :, None]
        outs.append((c - prev) / cnt - uf[:, :, gi])
    pooled = jnp.stack(outs, axis=2).astype(u.dtype)
    y = jnp.einsum('blgc,gcd->blgd', pooled, w_pool).reshape(B, L, POOL_WIDTH)
    return y * scale

def causal_dwconv(h, w, b):
    L = h.shape[1]
    hp = jnp.pad(h, ((0, 0), (CONV_WIDTH - 1, 0), (0, 0)))
    y = b
    for i in range(CONV_WIDTH):
        y = y + hp[:, i:i + L] * w[i]
    return y

def setup_inputs(seed: int = 0) -> dict:
    key = jax.random.key(seed)
    ks = jax.random.split(key, 17)

    def nrm(k, shape, scale):
        return scale * jax.random.normal(k, shape, jnp.float32)

    return {
        "x": nrm(ks[0], (BATCH, SEQ, D_MODEL), 1.0),
        "meta_tokens": nrm(ks[1], (N_META, D_MODEL), 1.0),
        "attn_norm_g": 1.0 + nrm(ks[2], (DEPTH, D_MODEL), 0.02),
        "w_in": nrm(ks[3], (DEPTH, D_MODEL, IN_WIDTH), D_MODEL ** -0.5),
        "q_norm_g": 1.0 + nrm(ks[4], (DEPTH, HEAD_DIM), 0.02),
        "k_norm_g": 1.0 + nrm(ks[5], (DEPTH, HEAD_DIM), 0.02),
        "sinks": nrm(ks[6], (DEPTH, N_Q_HEADS), 0.5),
        "w_pool": nrm(ks[7], (DEPTH, N_POOL_GROUPS, POOL_GROUP, POOL_GROUP), POOL_GROUP ** -0.5),
        "pool_scale": 1.0 + nrm(ks[8], (DEPTH, POOL_WIDTH), 0.02),
        "w_out": nrm(ks[9], (DEPTH, MIX_WIDTH, D_MODEL), MIX_WIDTH ** -0.5),
        "ffn_norm_g": 1.0 + nrm(ks[10], (DEPTH, D_MODEL), 0.02),
        "w_gate": nrm(ks[11], (DEPTH, D_MODEL, D_FF), D_MODEL ** -0.5),
        "w_up": nrm(ks[12], (DEPTH, D_MODEL, D_FF), D_MODEL ** -0.5),
        "conv_w": nrm(ks[13], (DEPTH, CONV_WIDTH, D_FF), CONV_WIDTH ** -0.5),
        "conv_b": nrm(ks[14], (DEPTH, D_FF), 0.01),
        "w_down": nrm(ks[15], (DEPTH, D_FF, D_MODEL), D_FF ** -0.5),
    }

def reference(x, meta_tokens, attn_norm_g, w_in, q_norm_g, k_norm_g, sinks, w_pool,
              pool_scale, w_out, ffn_norm_g, w_gate, w_up, conv_w, conv_b, w_down):
    B = x.shape[0]
    meta = jnp.broadcast_to(meta_tokens.astype(x.dtype)[None], (B, N_META, x.shape[-1]))
    h = jnp.concatenate([meta, x], axis=1)
    L = h.shape[1]
    cos, sin = rope_tables(L)
    q_scale = HEAD_DIM ** -0.5
    splits = [ATTN_WIDTH, ATTN_WIDTH + KV_WIDTH, ATTN_WIDTH + 2 * KV_WIDTH]

    for l in range(DEPTH):
        xn = rms_norm(h, attn_norm_g[l])
        proj = xn @ w_in[l]
        q, k, v, u = jnp.split(proj, splits, axis=-1)
        q = q.reshape(B, L, N_Q_HEADS, HEAD_DIM)
        k = k.reshape(B, L, N_KV_HEADS, HEAD_DIM)
        v = v.reshape(B, L, N_KV_HEADS, HEAD_DIM)
        q = apply_rope(rms_norm(q, q_norm_g[l]), cos, sin) * q_scale
        k = apply_rope(rms_norm(k, k_norm_g[l]), cos, sin)
        attn = sliding_sink_attention(q, k, v, sinks[l])
        pool = multiscale_pool(u, w_pool[l], pool_scale[l])
        h = h + jnp.concatenate([attn, pool], axis=-1) @ w_out[l]

        xn = rms_norm(h, ffn_norm_g[l])
        g = causal_dwconv(xn @ w_gate[l], conv_w[l], conv_b[l])
        h = h + (jax.nn.gelu(g, approximate=False) * (xn @ w_up[l])) @ w_down[l]

    return h[:, N_META:]


_drawn_inputs = setup_inputs


def setup_inputs(seed=0):
    import zlib

    import numpy as np

    out = dict(_drawn_inputs(seed))
    spreads = {}
    factors = {'attn_norm_g': 3.397,
     'q_norm_g': 8.0,
     'k_norm_g': 8.0,
     'sinks': 8.0,
     'pool_scale': 3.806,
     'ffn_norm_g': 2.938,
     'conv_b': 8.0}
    for name, (base, spread) in spreads.items():
        noise = np.random.default_rng([zlib.crc32(name.encode()), seed]).standard_normal(out[name].shape)
        drawn = base * np.exp(spread * noise) if base else spread * noise
        out[name] = __import__('jax').numpy.asarray(drawn.astype(out[name].dtype))
    for name, factor in factors.items():
        out[name] = (out[name] * factor).astype(out[name].dtype)
    return out
```

```python
import concourse.bass as bass
from concourse import mybir
from contextlib import ExitStack

D_MODEL, SEQ, DEPTH = 1024, 512, 2
CHUNK, N_META, HEAD_DIM = 64, 16, 64
N_Q_HEADS, N_KV_HEADS = 8, 2
ATTN_WIDTH = N_Q_HEADS * HEAD_DIM
KV_WIDTH = N_KV_HEADS * HEAD_DIM
POOL_WIDTH = D_MODEL - ATTN_WIDTH
POOL_SIZES = (2, 4, 8, 16)
IN_WIDTH = ATTN_WIDTH + 2 * KV_WIDTH + POOL_WIDTH
D_FF = ((8 * D_MODEL // 3 + 127) // 128) * 128
EPS = 1e-6
ROPE_THETA = 10000.0

P = 128
L = N_META + SEQ
HALF = L // 2
KT = D_MODEL // P
FT = D_FF // P
FI = FT // 2
UC = 2 * P
PAD = max(POOL_SIZES)
NCH = SEQ // CHUNK
NB = NCH + 1
NKEY = N_META + 2 * CHUNK
NWIN = NCH - 1

U_KV, U_Q, U_U01, U_U23, U_POOL, U_OUT = 0, 1, 3, 4, 5, 6
U_FFN = U_OUT + D_MODEL // UC
U_DOWN = U_FFN + 2 * FI
DOWN_K = [(0, 8), (8, 16), (16, FT)]
UNITS = U_DOWN + len(DOWN_K) * (D_MODEL // UC)

R_AG, R_FG, R_PS, R_CW = 0, KT, 2 * KT, 2 * KT + 4
R_CB = R_CW + 3 * FT
R_QG, R_KG = R_CB + FT, R_CB + FT + 1
NPAR = R_KG + 1

C_ID, C_BLK, C_ONE, C_CNT, C_COS, C_SIN = 0, P, 2 * P, 3 * P, 3 * P + 4 * PAD, 3 * P + 4 * PAD + L
NCONST = C_SIN + L


class Psum:
    PROLOGUE = [2, 3, 2, 2]

    def __init__(self):
        self.at, self.uses = {}, [0, 0, 0, 0]
        order = [("k", 2), ("v", 3), ("attn_norm", 0), ("q0", 1), ("v_T", 0), ("k_sq", 3), ("q1", 2),
                 ("q0_sq", 0), ("q2", 1), ("q1_sq", 3), ("q3", 2), ("q2_sq", 0), ("u0", 1), ("q3_sq", 3),
                 ("u1", 2), ("u2", 1), ("u3", 0)]
        order += [(f"scores{b}", 1 - b % 2) for b in range(NB)] + [("pool2", 0), ("pool3", 1)]
        order += [(f"probs_T{b}", 2) for b in range(NB)]
        order += [("heads0", 3), ("pool0", 3), ("heads1", 3), ("pool1", 3)]
        order += [(f"heads{b}", 3) for b in range(2, NB)]
        order += [(f"out{t}", (2 + t) % 4) for t in range(KT)] + [("ffn_norm", 0)]
        order += [("gate0", 2), ("gate1", 3), ("up0", 0), ("up1", 1)] * FI
        order += [(f"down{t}", (2 + t) % 4) for t in range(KT)]
        for name, slot in order:
            self.at.setdefault(name, (slot, self.uses[slot]))
            self.uses[slot] += 1

    def slot(self, name):
        return self.at[name][0]

    def before(self, name, layer, turn=0):
        slot, n = self.at[name]
        return layer * self.uses[slot] + turn + (self.PROLOGUE[slot] + n)

    def before_last_layer(self, name, layer):
        slot, n = self.at[name]
        return layer * self.uses[slot] + (self.PROLOGUE[slot] + n - self.uses[slot])


def build_trunk(nc, x, meta_tokens, attn_norm_g, w_in, q_norm_g, k_norm_g, sinks, w_pool, pool_scale,
                w_out, ffn_norm_g, w_gate, w_up, conv_w, conv_b, w_down, const, out):
    f32, f32r = mybir.dt.float32, mybir.dt.float32r
    ALU, ACT, AX = mybir.AluOpType, mybir.ActivationFunctionType, mybir.AxisListType
    ps = Psum()

    with ExitStack() as ctx:
        def sb(stack, name, shape, dt=f32):
            return stack.enter_context(nc.sbuf_tensor(name, shape, dt))

        def sem(name):
            return ctx.enter_context(nc.semaphore(name))

        h = sb(ctx, "h", [P, KT, L])
        x_hi = sb(ctx, "x_hi", [P, KT, L], f32r)
        x_lo = sb(ctx, "x_lo", [P, KT, L], f32r)
        raw = [sb(ctx, f"raw{s}", [P, 8, UC]) for s in range(2)]
        w_hi = [sb(ctx, f"w_hi{s}", [P, 8, UC], f32r) for s in range(2)]
        w_lo = [sb(ctx, f"w_lo{s}", [P, 8, UC], f32r) for s in range(2)]
        cst = sb(ctx, "cst", [P, NCONST])
        ident = cst[:, C_ID:C_ID + P]
        block_mean = cst[:, C_BLK:C_BLK + P]
        all_mean = cst[:, C_ONE:C_ONE + P]
        pool_fix = cst[:, C_CNT:C_CNT + 4 * PAD].rearrange("p (g t) -> p g t", g=4)
        cos, sin = cst[:, C_COS:C_COS + L], cst[:, C_SIN:C_SIN + L]
        rinv = sb(ctx, "rinv", [P, L])
        sumsq = sb(ctx, "sumsq", [P, L])
        sq = sb(ctx, "sq", [P, 2, L])
        ms_work = sb(ctx, "ms_work", [P, L])
        par_all = sb(ctx, "par_all", [P, DEPTH, NPAR])
        sink_all = sb(ctx, "sink_all", [P, DEPTH, 4])
        par = sb(ctx, "par", [P, NPAR])
        nsink = sb(ctx, "nsink", [P, 4])
        eps = sb(ctx, "eps", [P, 1])

        with ExitStack() as sc:
            q_rot = sb(sc, "q_rot", [P, N_KV_HEADS, NB, 2 * CHUNK])
            k_dup = sb(sc, "k_dup", [P, N_KV_HEADS, L])
            v_T = sb(sc, "v_T", [P, L])
            v_win = sb(sc, "v_win", [P, NWIN, P])
            v_meta = sb(sc, "v_meta", [N_META, P])
            u_sb = sb(sc, "u_sb", [P, 2, PAD + L])
            run_a = sb(sc, "run_a", [P, PAD + L])
            run_b = sb(sc, "run_b", [P, PAD + L])
            pooled = sb(sc, "pooled", [P, 2, L])
            pool_hi = sb(sc, "pool_hi", [P, 2, L], f32r)
            pool_lo = sb(sc, "pool_lo", [P, 2, L], f32r)
            mix_hi = sb(sc, "mix_hi", [P, KT, L], f32r)
            mix_lo = sb(sc, "mix_lo", [P, KT, L], f32r)
            head = sb(sc, "head", [P, 3, L])
            head_sq = sb(sc, "head_sq", [P, L])
            sine = sb(sc, "sine", [P, L])
            rot_c = sb(sc, "rot_c", [P, L])
            rot_s = sb(sc, "rot_s", [P, L])
            k_win = sb(sc, "k_win", [P, N_KV_HEADS, NWIN, NKEY])
            probs = sb(sc, "probs", [P, 2, 4, NKEY])
            probs_win = sb(sc, "probs_win", [P, 2, 4 * P])
            probs_meta = sb(sc, "probs_meta", [N_META, 2, 4 * P])
            nmax = sb(sc, "nmax", [P, 2, 4])
            nm = sb(sc, "nm", [P, 2, 4])
            sink_arg = sb(sc, "sink_arg", [P, 2, 4])
            sink_exp = sb(sc, "sink_exp", [P, 2, 4])
            row_sum = sb(sc, "row_sum", [P, 2, 4])
            den = sb(sc, "den", [P, 2, 4])
            rden = sb(sc, "rden", [P, 2, 4])
        with ExitStack() as sc:
            m_hi = sb(sc, "m_hi", [P, FT, L], f32r)
            m_lo = sb(sc, "m_lo", [P, FT, L], f32r)
            gate = [sb(sc, f"gate{c}", [P, 2 + L]) for c in range(2)]
            conv = [sb(sc, f"conv{c}", [P, L]) for c in range(2)]
            up = [sb(sc, f"up{c}", [P, L]) for c in range(2)]
            cpar = sb(sc, "cpar", [P, 4, 2])
        with ExitStack() as sc:
            x_in = sb(sc, "x_in", [P, SEQ // P, D_MODEL])
            meta_in = sb(sc, "meta_in", [N_META, D_MODEL])
            par_in = sb(sc, "par_in", [NPAR, DEPTH, P])
            sink_in = sb(sc, "sink_in", [P, DEPTH, 2, 2])
            y_out = sb(sc, "y_out", [P, SEQ // P, D_MODEL])

        slot = [ctx.enter_context(nc.psum_tensor(f"slot{s}", [P, 2, 512], f32)) for s in range(4)]

        def halves(s):
            return slot[s][:, :, 0:HALF]

        def tok(ap):
            return ap.rearrange("p (a t) -> p a t", a=2)

        x_loaded = [sem(f"x_loaded{t}") for t in range(SEQ // P)]
        meta_loaded, const_loaded, par_loaded = sem("meta_loaded"), sem("const_loaded"), sem("par_loaded")
        ident_loaded, sink_loaded = sem("ident_loaded"), sem("sink_loaded")
        raw_loaded = [sem("raw_loaded0"), sem("raw_loaded1")]
        hi_split = [sem("hi_split0"), sem("hi_split1")]
        lo_split = [sem("lo_split0"), sem("lo_split1")]
        down_used = sem("down_used")
        filled = [sem(f"filled{s}") for s in range(4)]
        evac = [sem(f"evac{s}") for s in range(4)]
        eps_ready = sem("eps_ready")
        par_ready = sem("par_ready")
        xhi_ready, xlo_ready = sem("xhi_ready"), sem("xlo_ready")
        sq_ready = sem("sq_ready")
        sq_added = sem("sq_added")
        run_ready = sem("run_ready")
        pooled_ready = sem("pooled_ready")
        phi_ready, plo_ready = sem("phi_ready"), sem("plo_ready")
        headsq_ready = sem("headsq_ready")
        headn_ready = sem("headn_ready")
        sine_ready = sem("sine_ready")
        rots_ready = sem("rots_ready")
        q_ready = sem("q_ready")
        k_ready = sem("k_ready")
        kwin_ready = sem("kwin_ready")
        nm_ready = sem("nm_ready")
        probs_ready = sem("probs_ready")
        meta_out = sem("meta_out")
        mixhi_ready = sem("mixhi_ready")
        tap2_ready = sem("tap2_ready")
        conv_ready = sem("conv_ready")
        gelu_ready = sem("gelu_ready")
        m_ready = sem("m_ready")
        mhi_ready, mlo_ready = sem("mhi_ready"), sem("mlo_ready")
        dve_par, dve_rot, dve_attn, dve_ffn = sem("dve_par"), sem("dve_rot"), sem("dve_attn"), sem("dve_ffn")
        pool_run, pool_rot, act_log = sem("pool_run"), sem("pool_rot"), sem("act_log")
        y_ready, y_stored = [sem("y_ready0"), sem("y_ready1")], [sem("y_stored0"), sem("y_stored1")]

        MIX_ORDER = ["heads0", "pool0", "heads1", "pool1"] + [f"heads{b}" for b in range(2, NB - 1)]
        MIX_ORDER += ["pool2", "pool3", f"heads{NB - 1}"]

        def mix_count(l, name):
            return l * len(MIX_ORDER) + (MIX_ORDER.index(name) + 1)

        class Chain:
            def __init__(self, eng, semaphore, turn, per):
                self.eng, self.sem, self.base, self.per, self.n = eng, semaphore, turn * per, per, 0

            def link(self, ins):
                self.n += 1
                ins.then_inc(self.sem, 1)
                self.eng.wait_ge(self.sem, self.base + self.n)

            def close(self):
                assert self.n == self.per, (self.n, self.per)

        def slot_turn(l, unit, pairs=0):
            return l * (UNITS // 2) + pairs + unit // 2

        def unit_rows(unit):
            if unit == U_POOL:
                return 2
            if unit >= U_DOWN:
                a, b = DOWN_K[(unit - U_DOWN) % 3]
                return b - a
            return 8

        def last_user_done(l, unit, i=0):
            old = unit - 2
            if old < 0:
                if old + UNITS == UNITS - 1:
                    name = f"down{KT - 1}"
                    return filled[ps.slot(name)], ps.before_last_layer(name, l) + 1
                return down_used, l * KT + 1
            if old >= U_DOWN:
                j, n = divmod(old - U_DOWN, 3)
                if n < 2:
                    return down_used, l * KT + (2 * j + n + 2)
                name = f"down{2 * j + 1}"
            elif old >= U_FFN:
                name = "gate1" if old == U_FFN else "up1"
            elif old >= U_OUT:
                name = f"out{2 * (old - U_OUT) + 1}"
            else:
                name = ("v", "q1", "q3", "u1", "u3", "pool3")[old]
            return filled[ps.slot(name)], ps.before(name, l, i) + 1

        def split_hi(act, l, unit, i=0):
            s, t, nk = unit % 2, slot_turn(l, unit, i), unit_rows(unit)
            act.wait_ge(*last_user_done(l, unit, i))
            act.wait_ge(raw_loaded[s], t * 32 + 32)
            nc.scalar.activation(w_hi[s][:, 0:nk], raw[s][:, 0:nk], ACT.Copy).then_inc(hi_split[s], 1)

        def split_lo(dve, l, unit, i=0):
            s, t, nk = unit % 2, slot_turn(l, unit, i), unit_rows(unit)
            dve.wait_ge(hi_split[s], t + 1)
            nc.vector.tensor_tensor(w_lo[s][:, 0:nk], raw[s][:, 0:nk], w_hi[s][:, 0:nk].bitcast(f32),
                                    ALU.subtract).then_inc(lo_split[s], 1)

        def h_from_layer_before(l, k):
            name = f"down{k}"
            return evac[ps.slot(name)], ps.before_last_layer(name, l) + 1

        def blocks(weights):
            return weights.rearrange("(k p) c -> p k c", p=P)

        BLOCKS = [(0, N_META), (N_META, N_META + CHUNK)] + [(N_META + c * CHUNK, NKEY) for c in range(1, NCH)]

        block = ctx.enter_context(nc.Block())

        @block.sync
        def _(sp):
            sp.dma_start(cst[:, 0:C_CNT], const[:, 0:C_CNT]).then_inc(ident_loaded, 16)
            for t in range(SEQ // P):
                sp.dma_start(x_in[:, t], x[0, t * P:(t + 1) * P, :]).then_inc(x_loaded[t], 16)

            def load(l, unit, src, i=0):
                s, n = unit % 2, unit_rows(unit)
                parts = [(raw[s][:, a:a + n // 2], src[:, a:a + n // 2]) for a in (n // 2, 0)]
                sp.wait_ge(lo_split[s], slot_turn(l, unit, i) + 1)
                for dst, part in parts:
                    sp.dma_start(dst, part).then_inc(raw_loaded[s], 16)

            with sp.Fori(0, DEPTH) as l:
                win, wo, wd = blocks(w_in[l]), blocks(w_out[l]), blocks(w_down[l])
                wg, wu = blocks(w_gate[l]), blocks(w_up[l])
                load(l, U_KV, win[:, :, ATTN_WIDTH:ATTN_WIDTH + UC])
                for j in range(2):
                    load(l, U_Q + j, win[:, :, j * UC:(j + 1) * UC])
                col_u = ATTN_WIDTH + 2 * KV_WIDTH
                load(l, U_U01, win[:, :, col_u:col_u + UC])
                load(l, U_U23, win[:, :, col_u + UC:col_u + 2 * UC])
                s = U_POOL % 2
                sp.wait_ge(lo_split[s], slot_turn(l, U_POOL) + 1)
                flat = w_pool.rearrange("l g c d -> (l g c) d")
                for g in range(2):
                    rows = flat[bass.ds(l * (4 * P) + g * (2 * P), 2 * P)]
                    sp.dma_start(raw[s][:, g].rearrange("p (g d) -> p g d", g=2),
                                 rows.rearrange("(g c) d -> c g d", g=2)).then_inc(raw_loaded[s], 16)
                for j in range(D_MODEL // UC):
                    load(l, U_OUT + j, wo[:, :, j * UC:(j + 1) * UC])
                with sp.Fori(0, FI) as i:
                    load(l, U_FFN, wg[:, :, bass.ds(i * UC, UC)], i)
                    load(l, U_FFN + 1, wu[:, :, bass.ds(i * UC, UC)], i)
                for j in range(D_MODEL // UC):
                    for n, (a, b) in enumerate(DOWN_K):
                        load(l, U_DOWN + 3 * j + n, wd[:, a:b, j * UC:(j + 1) * UC])
            for t in range(SEQ // P):
                for half in range(2):
                    sp.wait_ge(y_ready[half], t + 1)
                    cols = slice(half * 512, (half + 1) * 512)
                    sp.dma_start(out[0, t * P:(t + 1) * P, cols], y_out[:, t, cols]).then_inc(y_stored[half], 16)
            for half in range(2):
                sp.wait_ge(y_stored[half], 16 * (SEQ // P))

        @block.tensor
        def _(pe):
            def open_slot(name, l, turn=0):
                s = ps.slot(name)
                pe.wait_ge(evac[s], ps.before(name, l, turn))
                return s

            def dense(s, ws, col, rows, a_hi, a_lo, first=True, last=True, ready=None):
                for n, (r, k) in enumerate(rows):
                    if ready is not None:
                        ready(k)
                    end = last and n == len(rows) - 1
                    cols = slice(col, col + P)
                    for w, a in ((w_hi, a_hi), (w_hi, a_lo), (w_lo, a_hi)):
                        for half in range(2):
                            ins = nc.tensor.matmul(slot[s][:, half, 0:HALF], w[ws][:, r, cols],
                                                   a[:, k, half * HALF:(half + 1) * HALF],
                                                   start=first and n == 0 and w is w_hi and a is a_hi,
                                                   stop=end and w is w_lo)
                return ins

            def column_mean(name, l, weights, src, semaphore, count):
                s = open_slot(name, l)
                pe.wait_ge(semaphore, count)
                for half in range(2):
                    ins = nc.tensor.matmul(slot[s][:, half, 0:HALF], weights, src[:, half * HALF:(half + 1) * HALF],
                                           start=True, stop=True)
                ins.then_inc(filled[s], 1)

            pe.sem_inc(down_used, 1)
            pe.wait_ge(ident_loaded, 16)
            pe.wait_ge(meta_loaded, 16)
            for k in range(KT):
                s, feat = (2 + k) % 4, slice(k * P, (k + 1) * P)
                if k == 3:
                    pe.wait_ge(par_loaded, 16 * 11)
                    for l in range(DEPTH):
                        ins = nc.tensor.transpose(slot[s][:, l, 0:NPAR], par_in[:, l, :], ident[0:NPAR, 0:NPAR])
                    ins.then_inc(filled[s], 1)
                    pe.wait_ge(evac[s], 1)
                if k >= 4:
                    pe.wait_ge(evac[s], ps.PROLOGUE[s] - 1)
                nc.tensor.transpose(slot[s][:, 0, 0:N_META], meta_in[:, feat], ident[0:N_META, 0:N_META])
                for t in range(SEQ // P):
                    if k == 0:
                        pe.wait_ge(x_loaded[t], 16)
                    dst = slot[s][:, 0, N_META + t * P:N_META + (t + 1) * P] if t < 3 else slot[s][:, 1, 0:P]
                    ins = nc.tensor.transpose(dst, x_in[:, t, feat], ident)
                ins.then_inc(filled[s], 1)

            eight = [(k, k) for k in range(KT)]
            with pe.Fori(0, DEPTH) as l:
                def project(name, unit, ready=None):
                    c = int(name in ("v", "u1", "u3", "q1", "q3"))
                    s = open_slot(name, l)
                    if c == 0:
                        pe.wait_ge(lo_split[unit % 2], slot_turn(l, unit) + 2)
                    dense(s, unit % 2, c * P, eight, x_hi, x_lo, ready=ready).then_inc(filled[s], 1)

                def head_mean(name, e):
                    column_mean(name, l, block_mean, head_sq, headsq_ready, l * 5 + (e + 1))

                project("k", U_KV, ready=lambda k: pe.wait_ge(xlo_ready, l * (2 * KT) + (k + 1)))
                project("v", U_KV)
                column_mean("attn_norm", l, all_mean, sumsq, sq_added, l * (2 * (KT - 1)) + (KT - 1))
                project("q0", U_Q)
                s = open_slot("v_T", l)
                pe.wait_ge(evac[ps.slot("v")], ps.before("v", l) + 1)
                flat = slot[s][:].rearrange("p a t -> p (a t)")
                for w in range(NWIN):
                    t0 = N_META + w * CHUNK
                    nc.tensor.transpose(flat[:, w * P:(w + 1) * P], v_T[:, t0:t0 + P], ident)
                nc.tensor.transpose(flat[0:N_META, NWIN * P:(NWIN + 1) * P], v_T[:, 0:N_META], ident)\
                  .then_inc(filled[s], 1)
                head_mean("k_sq", 0)
                project("q1", U_Q)
                head_mean("q0_sq", 1)
                project("q2", U_Q + 1)
                head_mean("q1_sq", 2)
                project("q3", U_Q + 1)
                head_mean("q2_sq", 3)
                project("u0", U_U01)
                head_mean("q3_sq", 4)
                project("u1", U_U01)
                project("u2", U_U23)
                project("u3", U_U23)

                def pool_map(g):
                    s = open_slot(f"pool{g}", l)
                    if g == 0:
                        pe.wait_ge(lo_split[U_POOL % 2], slot_turn(l, U_POOL) + 2)
                    pe.wait_ge(plo_ready, l * 4 + (g + 1))
                    dense(s, U_POOL % 2, (g % 2) * P, [(g // 2, g % 2)], pool_hi, pool_lo).then_inc(filled[s], 1)

                def scores(b):
                    q0, nk = BLOCKS[b]
                    s = open_slot(f"scores{b}", l)
                    if b == 0:
                        pe.wait_ge(k_ready, l + 1)
                        pe.wait_ge(q_ready, l * 4 + 4)
                    if b == 2:
                        pe.wait_ge(kwin_ready, l + 1)
                    for t in range(4):
                        j2, kv = divmod(t, 2)
                        part = slice(j2 * HEAD_DIM, (j2 + 1) * HEAD_DIM)
                        keys = k_dup[part, kv, 0:nk] if b < 2 else k_win[part, kv, b - 2, :]
                        ins = nc.tensor.matmul(slot[s][:, j2, kv * nk:(kv + 1) * nk], q_rot[part, kv, b], keys,
                                               start=True, stop=True)
                    ins.then_inc(filled[s], 1)

                def probs_T(b):
                    nk = BLOCKS[b][1]
                    s = open_slot(f"probs_T{b}", l)
                    if b > 1:
                        pe.wait_ge(meta_out, l * (NB - 1) + (b - 1))
                    pe.wait_ge(probs_ready, l * NB + (b + 1))
                    for t in range(4):
                        ins = nc.tensor.transpose(slot[s][0:N_META, 1, t * P:(t + 1) * P],
                                                  probs[:, b % 2, t, 0:N_META], ident)
                        if nk > N_META:
                            ins = nc.tensor.transpose(slot[s][0:nk - N_META, 0, t * P:(t + 1) * P],
                                                      probs[:, b % 2, t, N_META:nk], ident)
                    ins.then_inc(filled[s], 1)

                def heads(b):
                    n = BLOCKS[b][1] - N_META
                    s = open_slot(f"heads{b}", l)
                    name = f"probs_T{b}"
                    pe.wait_ge(evac[ps.slot(name)], ps.before(name, l) + 1)
                    if b > 0:
                        pe.wait_ge(meta_out, l * (NB - 1) + b)
                    for t in range(4):
                        j2, kv = divmod(t, 2)
                        dst = slot[s][j2 * HEAD_DIM:(j2 + 1) * HEAD_DIM, 0, kv * P:(kv + 1) * P]
                        dims, cols = slice(kv * HEAD_DIM, (kv + 1) * HEAD_DIM), slice(t * P, (t + 1) * P)
                        ins = nc.tensor.matmul(dst, v_meta[:, dims], probs_meta[:, b % 2, cols],
                                               start=True, stop=n == 0)
                        if n > 0:
                            ins = nc.tensor.matmul(dst, v_win[0:n, max(b - 2, 0), dims], probs_win[0:n, b % 2, cols],
                                                   start=False, stop=True)
                    ins.then_inc(filled[s], 1)

                for step in range(NB + 2):
                    if step < NB:
                        scores(step)
                    if step == NB + 1:
                        pool_map(3)
                    if step >= 2:
                        heads(step - 2)
                    if 1 <= step <= NB:
                        probs_T(step - 1)
                    if step in (2, 3):
                        pool_map(step - 2)
                    if step == NB:
                        pool_map(2)

                rows = [(k, k) for k in (4, 5, 6, 7, 0, 1, 2, 3)]

                def mixed(k):
                    if k == 4:
                        pe.wait_ge(meta_out, l * (NB - 1) + (NB - 1))
                    if k >= 4:
                        name = f"pool{k - 4}"
                        pe.wait_ge(evac[ps.slot(name)], ps.before(name, l) + 1)
                    if k == 0:
                        name = f"heads{NB - 1}"
                        pe.wait_ge(evac[ps.slot(name)], ps.before(name, l) + 1)

                with pe.Fori(0, 2) as i:
                    for t in range(4):
                        s, unit = open_slot(f"out{t}", l, i), U_OUT + t // 2
                        if t % 2 == 0:
                            pe.wait_ge(lo_split[unit % 2], slot_turn(l, unit, i) + 2)
                        dense(s, unit % 2, (t % 2) * P, rows, mix_hi, mix_lo, ready=mixed if t == 0 else None)\
                          .then_inc(filled[s], 1)

                def mlp_tiles(i, ready=None):
                    for n, name in enumerate(("gate0", "gate1", "up0", "up1")):
                        s, unit = open_slot(name, l, i), U_FFN + n // 2
                        if n % 2 == 0:
                            pe.wait_ge(lo_split[unit % 2], slot_turn(l, unit, i) + 2)
                        dense(s, unit % 2, (n % 2) * P, eight, x_hi, x_lo,
                              ready=ready if n == 0 else None).then_inc(filled[s], 1)
                        if n == 0 and ready is not None:
                            column_mean("ffn_norm", l, all_mean, sumsq, sq_added,
                                        l * (2 * (KT - 1)) + 2 * (KT - 1))

                mlp_tiles(0, ready=lambda k: pe.wait_ge(xlo_ready, l * (2 * KT) + (KT + k + 1)))
                with pe.Fori(1, FI) as i:
                    mlp_tiles(i)
                with pe.Fori(0, 2) as i:
                    for j in range(2):
                        for n, (a, b) in enumerate(DOWN_K):
                            unit = U_DOWN + 3 * j + n
                            for c in range(2):
                                name = f"down{2 * j + c}"
                                s = open_slot(name, l, i) if n == 0 else ps.slot(name)
                                if c == 0:
                                    pe.wait_ge(lo_split[unit % 2], slot_turn(l, unit, i * 3) + 2)
                                    pe.wait_ge(mlo_ready, l * FT + b)
                                ins = dense(s, unit % 2, c * P, [(k - a, k) for k in range(a, b)],
                                            m_hi, m_lo, first=n == 0, last=n == 2)
                                if n == 2:
                                    ins.then_inc(filled[s], 1)
                                elif c == 1:
                                    ins.then_inc(down_used, 1)

            for s in range(4):
                pe.wait_ge(evac[s], ps.PROLOGUE[s] + ps.uses[s] * DEPTH)
            for t in range(SEQ // P):
                t0 = N_META + t * P
                for k in range(KT):
                    ins = nc.tensor.transpose(slot[t][:, k // 4, (k % 4) * P:(k % 4 + 1) * P], h[:, k, t0:t0 + P], ident)
                ins.then_inc(filled[t], 1)

        @block.gpsimd
        def _(pool):
            def sum_squares(norm):
                for k in range(1, KT):
                    pool.wait_ge(sq_ready, norm * KT + (k + 1))
                    if k == 1:
                        ins = nc.gpsimd.tensor_tensor(sumsq[:], sq[:, 0], sq[:, 1], ALU.add)
                    else:
                        pool.wait_ge(sq_added, norm * (KT - 1) + (k - 1))
                        ins = nc.gpsimd.tensor_tensor(sumsq[:], sumsq[:], sq[:, k % 2], ALU.add)
                    ins.then_inc(sq_added, 1)

            pool.wait_ge(const_loaded, 16)
            with pool.Fori(0, DEPTH) as l:
                sum_squares(l * 2)
                pads = Chain(pool, pool_run, l, 1)
                nc.gpsimd.memset(u_sb[:, :, 0:PAD], 0.0)
                nc.gpsimd.memset(run_a[:, 0:PAD], 0.0)
                pads.link(nc.gpsimd.memset(run_b[:, 0:PAD], 0.0))
                steps = Chain(pool, pool_rot, l, 10 + 5)

                def rotated(e):
                    pool.wait_ge(headn_ready, l * 5 + (e + 1))
                    if e == 1:
                        pool.wait_ge(k_ready, l + 1)
                    elif e > 1:
                        pool.wait_ge(q_ready, l * 4 + (e - 1))
                    steps.link(nc.gpsimd.tensor_tensor(rot_c[:], head[:, e % 3], cos, ALU.mult))
                    pool.wait_ge(rots_ready, l * 5 + (e + 1))
                    if e == 0:
                        for kv in range(N_KV_HEADS):
                            src = slice(kv * HEAD_DIM, (kv + 1) * HEAD_DIM)
                            for half in range(2):
                                ins = nc.gpsimd.tensor_tensor(k_dup[half * HEAD_DIM:(half + 1) * HEAD_DIM, kv],
                                                              rot_c[src], rot_s[src], ALU.add)
                        ins.then_inc(k_ready, 1)
                        return
                    kv, cols = (e - 1) // 2, slice((e - 1) % 2 * CHUNK, ((e - 1) % 2 + 1) * CHUNK)
                    chunks = [r[:, N_META:].rearrange("p (b q) -> p b q", q=CHUNK) for r in (rot_c, rot_s)]
                    nc.gpsimd.tensor_tensor(q_rot[:, kv, 0, cols], rot_c[:, 0:CHUNK], rot_s[:, 0:CHUNK], ALU.add)
                    nc.gpsimd.tensor_tensor(q_rot[:, kv, 1:, cols], *chunks, ALU.add).then_inc(q_ready, 1)

                def group(g):
                    pool.wait_ge(evac[ps.slot(f"u{g}")], ps.before(f"u{g}", l) + 1)
                    if g > 0:
                        pool.wait_ge(pooled_ready, l * 4 + g)
                    src, step = u_sb[:, g % 2], 1
                    for n in range(g + 1):
                        dst = (run_a, run_b)[(n + g) % 2]
                        steps.link(nc.gpsimd.tensor_tensor(dst[:, PAD:], src[:, PAD:],
                                                           src[:, PAD - step:PAD + L - step], ALU.add))
                        src, step = dst[:, :], step * 2
                    nc.gpsimd.tensor_tensor(run_a[:, PAD:2 * PAD], run_a[:, PAD:2 * PAD], pool_fix[:, g],
                                            ALU.mult).then_inc(run_ready, 1)

                for e in range(3):
                    rotated(e)
                group(0)
                rotated(3)
                group(1)
                rotated(4)
                group(2)
                group(3)
                steps.close()
                sum_squares(l * 2 + 1)
                with pool.Fori(0, FI) as i:
                    for c in range(2):
                        u = ps.slot(f"up{c}")
                        pool.wait_ge(gelu_ready, l * FT + i * 2 + (c + 1))
                        pool.wait_ge(evac[u], ps.before(f"up{c}", l, i) + 1)
                        nc.gpsimd.tensor_tensor(up[c][:], up[c][:], conv[c][:], ALU.mult).then_inc(m_ready, 1)

        @block.scalar
        def _(act):
            act.dma_start(meta_in[:], meta_tokens).then_inc(meta_loaded, 16)
            by_row = "l (r p) -> r l p"
            for src, r, n in ((attn_norm_g, R_AG, KT), (ffn_norm_g, R_FG, KT), (pool_scale, R_PS, 4),
                              (conv_b, R_CB, FT), (conv_w[:, 0], R_CW, FT), (conv_w[:, 1], R_CW + FT, FT),
                              (conv_w[:, 2], R_CW + 2 * FT, FT)):
                act.dma_start(par_in[r:r + n], src.rearrange(by_row, p=P)).then_inc(par_loaded, 16)
            for src, r in ((q_norm_g, R_QG), (k_norm_g, R_KG)):
                for half in range(2):
                    act.dma_start(par_in[r:r + 1, :, half * HEAD_DIM:(half + 1) * HEAD_DIM],
                                  src.rearrange("(a l) d -> a l d", a=1)).then_inc(par_loaded, 16)
            for l in range(DEPTH):
                for jp in range(2):
                    act.dma_start(sink_in[jp * 64:(jp + 1) * 64, l],
                                  sinks[l].rearrange("(kv jp j) -> jp kv j", jp=2, j=2)[jp]
                                  .partition_broadcast(64)).then_inc(sink_loaded, 16)
            act.dma_start(cst[:, C_CNT:], const[:, C_CNT:]).then_inc(const_loaded, 16)

            def gain_hi(k, ready, row):
                act.wait_ge(*ready)
                nc.scalar.activation(x_hi[:, k], h[:, k], ACT.Copy, scale=par[:, row + k:row + k + 1])\
                  .then_inc(xhi_ready, 1)

            act.wait_ge(eps_ready, 1)
            with act.Fori(0, DEPTH) as l:
                roots = Chain(act, act_log, l, 2)

                def square(norm, k):
                    if k >= 2:
                        act.wait_ge(sq_added, (l * 2 + norm) * (KT - 1) + max(1, k - 2))
                    nc.scalar.activation(sq[:, k % 2], h[:, k], ACT.Square).then_inc(sq_ready, 1)

                def root(name, dst):
                    s = ps.slot(name)
                    act.wait_ge(filled[s], ps.before(name, l) + 1)
                    roots.link(nc.scalar.activation(tok(ms_work[:]), halves(s), ACT.Ln, bias=eps[:]))
                    nc.scalar.activation(dst, ms_work[:], ACT.Exp, scale=-0.5).then_inc(evac[s], 1)

                def head_root(e):
                    if e > 0:
                        act.wait_ge(headn_ready, l * 5 + e)
                    name = "k_sq" if e == 0 else f"q{e - 1}_sq"
                    s = ps.slot(name)
                    act.wait_ge(filled[s], ps.before(name, l) + 1)
                    nc.scalar.activation(tok(ms_work[:]), halves(s), ACT.Sqrt, bias=eps[:]).then_inc(evac[s], 1)

                def head_square(e):
                    name = "k" if e == 0 else f"q{e - 1}"
                    act.wait_ge(evac[ps.slot(name)], ps.before(name, l) + 1)
                    nc.scalar.activation(head_sq[:], head[:, e % 3], ACT.Square).then_inc(headsq_ready, 1)

                def shift(e):
                    act.wait_ge(sine_ready, l * 5 + (e + 1))
                    if e == 1:
                        act.wait_ge(k_ready, l + 1)
                    elif e > 1:
                        act.wait_ge(q_ready, l * 4 + (e - 1))
                    for to, fr in ((0, 32), (32, 0), (64, 96), (96, 64)):
                        ins = nc.scalar.activation(rot_s[to:to + 32], sine[fr:fr + 32], ACT.Copy)
                    ins.then_inc(rots_ready, 1)

                def pooled_hi(g):
                    act.wait_ge(pooled_ready, l * 4 + (g + 1))
                    if g >= 2:
                        name = f"pool{g - 2}"
                        act.wait_ge(filled[ps.slot(name)], ps.before(name, l) + 1)
                    nc.scalar.activation(pool_hi[:, g % 2], pooled[:, g % 2], ACT.Copy).then_inc(phi_ready, 1)

                def pool_map_hi(g):
                    s = ps.slot(f"pool{g}")
                    act.wait_ge(filled[s], ps.before(f"pool{g}", l) + 1)
                    nc.scalar.activation(tok(mix_hi[:, 4 + g]), halves(s), ACT.Copy,
                                         scale=par[:, R_PS + g:R_PS + g + 1]).then_inc(mixhi_ready, 1)

                split_hi(act, l, 0)
                act.wait_ge(par_ready, l * 2 + 2)
                for k in range(KT):
                    gain_hi(k, h_from_layer_before(l, k), R_AG)
                split_hi(act, l, 1)
                for k in range(KT):
                    square(0, k)
                root("attn_norm", rinv[:])
                split_hi(act, l, 2)
                head_square(0)
                s = ps.slot("v_T")
                act.wait_ge(filled[s], ps.before("v_T", l) + 1)
                flat = slot[s][:].rearrange("p a t -> p (a t)")
                nc.scalar.activation(v_meta[:], flat[0:N_META, NWIN * P:(NWIN + 1) * P], ACT.Copy)
                nc.scalar.activation(v_win[:, 0:4].rearrange("p w d -> p (w d)"), flat[:, 0:4 * P], ACT.Copy)
                nc.scalar.activation(v_win[:, 4:NWIN].rearrange("p w d -> p (w d)"), flat[:, 4 * P:NWIN * P],
                                     ACT.Copy).then_inc(evac[s], 1)
                head_root(0)
                head_square(1)
                shift(0)
                head_root(1)
                head_square(2)
                split_hi(act, l, 3)
                shift(1)
                head_root(2)
                head_square(3)
                split_hi(act, l, 4)
                shift(2)
                act.wait_ge(k_ready, l + 1)
                for kv in range(N_KV_HEADS):
                    nc.scalar.activation(k_win[:, kv, :, 0:N_META],
                                         k_dup[:, kv, 0:N_META].unsqueeze(1).broadcast_to([P, NWIN, N_META]), ACT.Copy)
                    keys = k_dup[:, kv, N_META:]
                    windows = bass.AP(keys.tensor, keys.offset, [list(keys.ap[0]), [CHUNK, NWIN], [1, 2 * CHUNK]])
                    ins = nc.scalar.activation(k_win[:, kv, :, N_META:], windows, ACT.Copy)
                ins.then_inc(kwin_ready, 1)
                head_root(3)
                head_square(4)
                shift(3)
                split_hi(act, l, 5)
                head_root(4)
                shift(4)
                pooled_hi(0)
                pooled_hi(1)

                def exps(b):
                    nk, s, y = BLOCKS[b][1], ps.slot(f"scores{b}"), b % 2
                    act.wait_ge(nm_ready, l * NB + b + 1)
                    if b >= 2:
                        old = f"probs_T{b - 2}"
                        act.wait_ge(filled[ps.slot(old)], ps.before(old, l) + 1)
                    nc.scalar.activation(sink_exp[:, y], sink_arg[:, y], ACT.Exp)
                    for t in range(4):
                        col = slice((t % 2) * nk, (t % 2 + 1) * nk)
                        ins = nc.scalar.activation(probs[:, y, t, 0:nk], slot[s][:, t // 2, col], ACT.Exp,
                                                   bias=nm[:, y, t:t + 1], accum_out=row_sum[:, y, t:t + 1])
                    ins.then_inc(evac[s], 1)

                def probs_out(b):
                    n = BLOCKS[b][1] - N_META
                    pt = ps.slot(f"probs_T{b}")
                    act.wait_ge(filled[pt], ps.before(f"probs_T{b}", l) + 1)
                    if n > 0:
                        ins = nc.scalar.activation(probs_win[0:n, b % 2], slot[pt][0:n, 0, :], ACT.Copy)
                    else:
                        ins = nc.scalar.activation(probs_meta[:, 0], slot[pt][0:N_META, 1, :], ACT.Copy)
                    ins.then_inc(evac[pt], 1)

                def heads_hi(b):
                    t0, nq = BLOCKS[b][0], CHUNK if b else N_META
                    hd = ps.slot(f"heads{b}")
                    act.wait_ge(filled[hd], ps.before(f"heads{b}", l) + 1)
                    src = slot[hd][:, 0, 0:4 * CHUNK].rearrange("p (t q) -> p t q", t=4)[:, :, 0:nq]
                    nc.scalar.activation(mix_hi[:, 0:4, t0:t0 + nq], src, ACT.Copy).then_inc(mixhi_ready, 1)

                for step in range(NB + 2):
                    if step < NB:
                        exps(step)
                    if step == NB + 1:
                        pool_map_hi(3)
                    if step >= 2:
                        heads_hi(step - 2)
                    if 1 <= step <= NB:
                        probs_out(step - 1)
                    if step in (2, 3):
                        pool_map_hi(step - 2)
                    if step in (4, 6):
                        pooled_hi(step // 2)
                    if step == 5:
                        split_hi(act, l, U_OUT)
                    if step == NB:
                        pool_map_hi(2)
                split_hi(act, l, U_OUT + 1)

                for j in range(4):
                    if j < 3:
                        split_hi(act, l, U_OUT + 2 + j)
                    for k in (2 * j, 2 * j + 1):
                        gain_hi(k, (evac[ps.slot(f"out{k}")], ps.before(f"out{k}", l) + 1), R_FG)
                        square(1, k)
                split_hi(act, l, U_OUT + 5)
                root("ffn_norm", rinv[:])
                roots.close()

                with act.Fori(0, FI) as i:
                    for c in range(2):
                        g = ps.slot(f"gate{c}")
                        act.wait_ge(evac[g], ps.before(f"gate{c}", l, i) + 1)
                        nc.scalar.activation(conv[c][:], gate[c][:, 2:], ACT.Identity, bias=cpar[:, 3, c:c + 1],
                                             scale=cpar[:, 2, c:c + 1]).then_inc(tap2_ready, 1)
                    split_hi(act, l, U_FFN + 2, i)
                    for c in range(2):
                        act.wait_ge(conv_ready, l * FT + i * 2 + (c + 1))
                        nc.scalar.activation(conv[c][:], conv[c][:], ACT.Gelu).then_inc(gelu_ready, 1)
                    split_hi(act, l, U_FFN + 3, i)
                    for c in range(2):
                        act.wait_ge(m_ready, l * FT + i * 2 + (c + 1))
                        nc.scalar.activation(m_hi[:, bass.ds(i * 2 + c, 1)].rearrange("p a t -> p (a t)"),
                                             up[c][:], ACT.Copy).then_inc(mhi_ready, 1)
                for unit in range(U_DOWN + 2, UNITS):
                    split_hi(act, l, unit)

            for t in range(SEQ // P):
                act.wait_ge(filled[t], ps.PROLOGUE[t] + ps.uses[t] * DEPTH + 1)
                nc.scalar.activation(y_out[:, t, 0:512], slot[t][:, 0, :], ACT.Copy).then_inc(y_ready[0], 1)

        @block.vector
        def _(dve):
            for s in range(2):
                dve.sem_inc(lo_split[s], 1)
            nc.vector.memset(eps[:], EPS).then_inc(eps_ready, 1)
            for k in range(KT):
                s, cut = (2 + k) % 4, N_META + 3 * P
                if k == 3:
                    dve.wait_ge(filled[s], 1)
                    nc.vector.tensor_copy(par_all[:], slot[s][:, :, 0:NPAR]).then_inc(evac[s], 1)
                dve.wait_ge(filled[s], ps.PROLOGUE[s] - (k < 4))
                nc.vector.tensor_copy(h[:, k, 0:cut], slot[s][:, 0, 0:cut])
                nc.vector.tensor_copy(h[:, k, cut:L], slot[s][:, 1, 0:P]).then_inc(evac[s], 1)
            dve.wait_ge(evac[1], 1)
            dve.wait_ge(sink_loaded, 16 * 2 * DEPTH)
            prep = Chain(dve, dve_par, 0, 2)
            prep.link(nc.vector.tensor_scalar(sink_all[:].rearrange("p l (j kv) -> p l j kv", j=2),
                                              sink_in[:].rearrange("p l kv j -> p l j kv"), -1.0, None, ALU.mult))
            prep.link(nc.vector.tensor_scalar(par_all[:, :, R_QG:R_QG + 1], par_all[:, :, R_QG:R_QG + 1],
                                              float(HEAD_DIM) ** -0.5, None, ALU.mult))
            prep.close()
            dve.wait_ge(const_loaded, 16)

            def gain_lo(k, count, row):
                dve.wait_ge(xhi_ready, count)
                nc.vector.scalar_tensor_tensor(x_lo[:, k], h[:, k], par[:, row + k:row + k + 1],
                                               x_hi[:, k].bitcast(f32), ALU.mult, ALU.subtract)\
                  .then_inc(xlo_ready, 1)

            with dve.Fori(0, DEPTH) as l:
                nc.vector.tensor_copy(par[:], par_all[:, bass.ds(l, 1)].rearrange("p a r -> p (a r)"))\
                  .then_inc(par_ready, 1)
                nc.vector.tensor_copy(nsink[:], sink_all[:, bass.ds(l, 1)].rearrange("p a r -> p (a r)"))\
                  .then_inc(par_ready, 1)
                split_lo(dve, l, 0)
                dve.wait_ge(par_ready, l * 2 + 2)
                for k in range(KT):
                    gain_lo(k, l * (2 * KT) + (k + 1), R_AG)
                split_lo(dve, l, 1)

                def inverse_rms_ready(name):
                    dve.wait_ge(evac[ps.slot(name)], ps.before(name, l) + 1)

                def scaled(name, dst, turn=0):
                    s = ps.slot(name)
                    dve.wait_ge(filled[s], ps.before(name, l, turn) + 1)
                    nc.vector.tensor_tensor(tok(dst), halves(s), tok(rinv[:]), ALU.mult).then_inc(evac[s], 1)

                def head_tile(e):
                    if e == 3:
                        dve.wait_ge(k_ready, l + 1)
                    if e == 4:
                        dve.wait_ge(q_ready, l * 4 + 1)
                    scaled("k" if e == 0 else f"q{e - 1}", head[:, e % 3])

                rot = Chain(dve, dve_rot, l, 5)

                def rotate(e):
                    tile, row = head[:, e % 3], R_KG if e == 0 else R_QG
                    name = "k_sq" if e == 0 else f"q{e - 1}_sq"
                    dve.wait_ge(evac[ps.slot(name)], ps.before(name, l) + 1)
                    rot.link(nc.vector.reciprocal(ms_work[:], ms_work[:]))
                    nc.vector.scalar_tensor_tensor(tile, tile, par[:, row:row + 1], ms_work[:],
                                                   ALU.mult, ALU.mult).then_inc(headn_ready, 1)
                    dve.wait_ge(headn_ready, l * 5 + (e + 1))
                    if e > 0:
                        dve.wait_ge(rots_ready, l * 5 + e)
                    nc.vector.tensor_tensor(sine[:], tile, sin, ALU.mult).then_inc(sine_ready, 1)

                def pooled_tile(g):
                    dve.wait_ge(run_ready, l * 4 + (g + 1))
                    if g >= 2:
                        dve.wait_ge(plo_ready, l * 4 + (g - 1))
                    nc.vector.scalar_tensor_tensor(pooled[:, g % 2], run_a[:, PAD:], 1.0 / POOL_SIZES[g],
                                                   u_sb[:, g % 2, PAD:], ALU.mult, ALU.subtract)\
                      .then_inc(pooled_ready, 1)

                def pooled_lo(g):
                    dve.wait_ge(phi_ready, l * 4 + (g + 1))
                    nc.vector.tensor_tensor(pool_lo[:, g % 2], pooled[:, g % 2], pool_hi[:, g % 2].bitcast(f32),
                                            ALU.subtract).then_inc(plo_ready, 1)

                inverse_rms_ready("attn_norm")
                head_tile(0)
                scaled("v", v_T[:])
                split_lo(dve, l, 2)
                head_tile(1)
                rotate(0)
                head_tile(2)
                rotate(1)
                split_lo(dve, l, 3)
                head_tile(3)
                rotate(2)
                head_tile(4)
                split_lo(dve, l, 4)
                rotate(3)
                scaled("u0", u_sb[:, 0, PAD:])
                rotate(4)
                rot.close()
                pooled_tile(0)
                scaled("u1", u_sb[:, 1, PAD:])
                split_lo(dve, l, 5)
                dve.wait_ge(pooled_ready, l * 4 + 1)
                scaled("u2", u_sb[:, 0, PAD:])
                pooled_lo(0)
                pooled_tile(1)
                dve.wait_ge(pooled_ready, l * 4 + 2)
                scaled("u3", u_sb[:, 1, PAD:])
                pooled_lo(1)

                def pool_map_lo(g):
                    s = ps.slot(f"pool{g}")
                    dve.wait_ge(mixhi_ready, mix_count(l, f"pool{g}"))
                    nc.vector.scalar_tensor_tensor(tok(mix_lo[:, 4 + g]), halves(s), par[:, R_PS + g:R_PS + g + 1],
                                                   tok(mix_hi[:, 4 + g].bitcast(f32)), ALU.mult, ALU.subtract)\
                      .then_inc(evac[s], 1)

                ch = Chain(dve, dve_attn, l, 4 * NB)

                def row_maxima(b):
                    nk, s, y = BLOCKS[b][1], ps.slot(f"scores{b}"), b % 2
                    dve.wait_ge(filled[s], ps.before(f"scores{b}", l) + 1)
                    view = slot[s][:, :, 0:2 * nk].rearrange("p a (t k) -> p a t k", t=2)
                    ch.link(nc.vector.tensor_reduce(nmax[:, y].rearrange("p (a t) -> p a t", a=2), view, op=ALU.max,
                                                    axis=AX.X, negate=True))
                    ch.link(nc.vector.tensor_tensor(nm[:, y], nmax[:, y], nsink[:], ALU.min))
                    nc.vector.tensor_tensor(sink_arg[:, y], nm[:, y], nsink[:], ALU.subtract).then_inc(nm_ready, 1)

                def divide(b):
                    nk, s, y = BLOCKS[b][1], ps.slot(f"scores{b}"), b % 2
                    dve.wait_ge(evac[s], ps.before(f"scores{b}", l) + 1)
                    ch.link(nc.vector.tensor_tensor(den[:, y], row_sum[:, y], sink_exp[:, y], ALU.add))
                    ch.link(nc.vector.reciprocal(rden[:, y], den[:, y]))
                    nc.vector.tensor_tensor(probs[:, y, :, 0:nk], probs[:, y, :, 0:nk],
                                            rden[:, y].unsqueeze(2).broadcast_to([P, 4, nk]), ALU.mult)\
                      .then_inc(probs_ready, 1)

                def meta_probs_out(b):
                    pt = ps.slot(f"probs_T{b}")
                    dve.wait_ge(filled[pt], ps.before(f"probs_T{b}", l) + 1)
                    nc.vector.tensor_copy(probs_meta[:, b % 2], slot[pt][0:N_META, 1, :]).then_inc(meta_out, 1)

                def heads_lo(b):
                    t0, nq = BLOCKS[b][0], CHUNK if b else N_META
                    hd = ps.slot(f"heads{b}")
                    dve.wait_ge(mixhi_ready, mix_count(l, f"heads{b}"))
                    src = slot[hd][:, 0, 0:4 * CHUNK].rearrange("p (t q) -> p t q", t=4)[:, :, 0:nq]
                    nc.vector.tensor_tensor(mix_lo[:, 0:4, t0:t0 + nq], src,
                                            mix_hi[:, 0:4, t0:t0 + nq].bitcast(f32), ALU.subtract)\
                      .then_inc(evac[hd], 1)

                for step in range(NB + 2):
                    if step < NB:
                        row_maxima(step)
                        divide(step)
                    if step == NB + 1:
                        pool_map_lo(3)
                    if step >= 2:
                        heads_lo(step - 2)
                    if 2 <= step <= NB:
                        meta_probs_out(step - 1)
                    if step in (2, 3):
                        pool_map_lo(step - 2)
                    if step in (3, 5):
                        pooled_tile((step + 1) // 2)
                    if step in (5, 7):
                        pooled_lo((step - 1) // 2)
                    if step == 6:
                        split_lo(dve, l, U_OUT)
                    if step == NB:
                        pool_map_lo(2)
                ch.close()
                split_lo(dve, l, U_OUT + 1)

                def add_to_h(name, k):
                    s = ps.slot(name)
                    dve.wait_ge(filled[s], ps.before(name, l) + 1)
                    nc.vector.tensor_tensor(tok(h[:, k]), halves(s), tok(h[:, k]), ALU.add).then_inc(evac[s], 1)

                for j in range(4):
                    for k in (2 * j, 2 * j + 1):
                        add_to_h(f"out{k}", k)
                    if j < 3:
                        split_lo(dve, l, U_OUT + 2 + j)
                    for k in (2 * j, 2 * j + 1):
                        gain_lo(k, l * (2 * KT) + (KT + k + 1), R_FG)
                split_lo(dve, l, U_OUT + 5)

                inverse_rms_ready("ffn_norm")
                for c in range(2):
                    nc.vector.memset(gate[c][:, 0:2], 0.0)
                taps = par[:, R_CW:R_CW + 4 * FT].rearrange("p (t f) -> p t f", t=4)
                with dve.Fori(0, FI) as i:
                    ch = Chain(dve, dve_ffn, l * FI + i, 3)
                    ch.link(nc.vector.tensor_copy(cpar[:], taps[:, :, bass.ds(i * 2, 2)]))
                    for c in range(2):
                        scaled(f"gate{c}", gate[c][:, 2:], i)
                    split_lo(dve, l, U_FFN + 2, i)
                    for c in range(2):
                        dve.wait_ge(tap2_ready, l * FT + i * 2 + (c + 1))
                        ch.link(nc.vector.scalar_tensor_tensor(conv[c][:], gate[c][:, 1:1 + L], cpar[:, 1, c:c + 1],
                                                               conv[c][:], ALU.mult, ALU.add))
                        nc.vector.scalar_tensor_tensor(conv[c][:], gate[c][:, 0:L], cpar[:, 0, c:c + 1],
                                                       conv[c][:], ALU.mult, ALU.add).then_inc(conv_ready, 1)
                    ch.close()
                    for c in range(2):
                        scaled(f"up{c}", up[c][:], i)
                    split_lo(dve, l, U_FFN + 3, i)
                    for c in range(2):
                        dve.wait_ge(mhi_ready, l * FT + i * 2 + (c + 1))
                        one = bass.ds(i * 2 + c, 1)
                        nc.vector.tensor_tensor(m_lo[:, one].rearrange("p a t -> p (a t)"), up[c][:],
                                                m_hi[:, one].rearrange("p a t -> p (a t)").bitcast(f32),
                                                ALU.subtract).then_inc(mlo_ready, 1)
                for j in range(4):
                    for n in range(3):
                        unit = U_DOWN + 3 * j + n
                        if n == 2:
                            for k in (2 * j, 2 * j + 1):
                                add_to_h(f"down{k}", k)
                        if unit + 2 < UNITS:
                            split_lo(dve, l, unit + 2)

            for t in range(SEQ // P):
                dve.wait_ge(filled[t], ps.PROLOGUE[t] + ps.uses[t] * DEPTH + 1)
                nc.vector.tensor_copy(y_out[:, t, 512:], slot[t][:, 1, :]).then_inc(y_ready[1], 1)


def constant_table():
    import numpy as np

    table = np.zeros((P, NCONST), np.float32)
    table[:, C_ID:C_ID + P] = np.eye(P, dtype=np.float32)
    heads = np.arange(P) // HEAD_DIM
    table[:, C_BLK:C_BLK + P] = (heads[:, None] == heads[None, :]).astype(np.float32) / HEAD_DIM
    table[:, C_ONE:C_ONE + P] = 1.0 / D_MODEL
    t = np.arange(PAD)
    for g, w in enumerate(POOL_SIZES):
        table[:, C_CNT + g * PAD:C_CNT + (g + 1) * PAD] = w / np.minimum(t + 1, w)
    half = HEAD_DIM // 2
    inv = (1.0 / (np.float32(ROPE_THETA) ** (np.arange(0, HEAD_DIM, 2, dtype=np.float32) / np.float32(HEAD_DIM))))
    angle = np.arange(L, dtype=np.float32)[None, :] * inv.astype(np.float32)[:, None]
    feature = np.arange(P) % half
    sign = np.where(np.arange(P) % HEAD_DIM < half, 1.0, -1.0).astype(np.float32)
    table[:, C_COS:C_COS + L] = np.cos(angle)[feature]
    table[:, C_SIN:C_SIN + L] = np.sin(angle)[feature] * sign[:, None]
    return table


_INS = ["x", "meta_tokens", "attn_norm_g", "w_in", "q_norm_g", "k_norm_g", "sinks", "w_pool", "pool_scale",
        "w_out", "ffn_norm_g", "w_gate", "w_up", "conv_w", "conv_b", "w_down"]


def kernel(**inputs):
    import numpy as _np
    import concourse.bacc as _bacc
    from concourse.bass_utils import run_bass_kernel_spmd as _run

    nc = _bacc.Bacc("TRN2", target_bir_lowering=False, num_devices=1, dynamic_dma_scratch_size=256)
    arrays, args = {}, []
    for name in _INS:
        a = _np.ascontiguousarray(inputs[name])
        arrays[f"in_{name}"] = a
        args.append(nc.dram_tensor(f"in_{name}", a.shape, mybir.dt.from_np(a.dtype), kind="ExternalInput").ap())
    table = constant_table()
    arrays["const_table"] = table
    args.append(nc.dram_tensor("const_table", table.shape, mybir.dt.float32, kind="ExternalInput").ap())
    args.append(nc.dram_tensor("out", (1, SEQ, D_MODEL), mybir.dt.float32, kind="ExternalOutput").ap())
    build_trunk(nc, *args)
    result = _run(nc, [arrays], core_ids=[0])
    return result.results[0]["out"]
```

```python
import concourse.bass as bass
from concourse import mybir
from contextlib import ExitStack

D_MODEL, SEQ, DEPTH = 1024, 512, 2
CHUNK, N_META, HEAD_DIM = 64, 16, 64
N_Q_HEADS, N_KV_HEADS = 8, 2
ATTN_WIDTH = N_Q_HEADS * HEAD_DIM
KV_WIDTH = N_KV_HEADS * HEAD_DIM
POOL_WIDTH = D_MODEL - ATTN_WIDTH
POOL_SIZES = (2, 4, 8, 16)
IN_WIDTH = ATTN_WIDTH + 2 * KV_WIDTH + POOL_WIDTH
D_FF = ((8 * D_MODEL // 3 + 127) // 128) * 128
EPS = 1e-6
ROPE_THETA = 10000.0

P = 128
L = N_META + SEQ
HALF = L // 2
KT = D_MODEL // P
FT = D_FF // P
FI = FT // 2
UC = 2 * P
PAD = max(POOL_SIZES)
NCH = SEQ // CHUNK
NB = NCH + 1
NKEY = N_META + 2 * CHUNK
NWIN = NCH - 1

U_KV, U_Q, U_U01, U_U23, U_POOL, U_OUT = 0, 1, 3, 4, 5, 6
U_FFN = U_OUT + D_MODEL // UC
U_DOWN = U_FFN + 2 * FI
DOWN_K = [(0, 8), (8, 16), (16, FT)]
UNITS = U_DOWN + len(DOWN_K) * (D_MODEL // UC)

R_AG, R_FG, R_PS, R_CW = 0, KT, 2 * KT, 2 * KT + 4
R_CB = R_CW + 3 * FT
R_QG, R_KG = R_CB + FT, R_CB + FT + 1
NPAR = R_KG + 1

C_ID, C_BLK, C_ONE, C_CNT, C_COS, C_SIN = 0, P, 2 * P, 3 * P, 3 * P + 4 * PAD, 3 * P + 4 * PAD + L
NCONST = C_SIN + L


class Psum:
    PROLOGUE = [2, 3, 2, 2, 0]

    def __init__(self):
        self.at, self.uses = {}, [0, 0, 0, 0, 0]
        order = [("k", 2), ("v", 3), ("attn_norm", 0), ("q0", 1), ("v_T", 0), ("k_sq", 3), ("q1", 2),
                 ("q2", 1), ("qn0", 0), ("q3", 3), ("u0", 2), ("qn1", 0)]
        order += [(f"scores{b}", 1 - b % 2) for b in range(NB)] + [("pool2", 0), ("pool3", 1)]
        order += [(f"probs_T{b}", 2) for b in range(NB)] + [(f"heads{b}", 3) for b in range(NB)]
        order += [(f"u{g}{half}", 4) for g in (1, 2, 3) for half in "ab"]
        order += [(f"pool{g}{half}", 4) for g in (0, 1) for half in "ab"]
        order += [(f"out{t}", (2 + t) % 4) for t in range(KT)] + [("ffn_norm", 0)]
        order += [("gate0", 2), ("gate1", 3), ("up0", 0), ("up1", 1)] * FI
        order += [(f"down{t}", (2 + t) % 4) for t in range(KT)]
        for name, slot in order:
            self.at.setdefault(name, (slot, self.uses[slot]))
            self.uses[slot] += 1

    def slot(self, name):
        return self.at[name][0]

    def before(self, name, layer, turn=0):
        slot, n = self.at[name]
        return layer * self.uses[slot] + turn + (self.PROLOGUE[slot] + n)

    def before_last_layer(self, name, layer):
        slot, n = self.at[name]
        return layer * self.uses[slot] + (self.PROLOGUE[slot] + n - self.uses[slot])


def build_trunk(nc, x, meta_tokens, attn_norm_g, w_in, q_norm_g, k_norm_g, sinks, w_pool, pool_scale,
                w_out, ffn_norm_g, w_gate, w_up, conv_w, conv_b, w_down, const, out):
    f32, f32r = mybir.dt.float32, mybir.dt.float32r
    ALU, ACT, AX = mybir.AluOpType, mybir.ActivationFunctionType, mybir.AxisListType
    ps = Psum()

    with ExitStack() as ctx:
        def sb(stack, name, shape, dt=f32):
            return stack.enter_context(nc.sbuf_tensor(name, shape, dt))

        def sem(name):
            return ctx.enter_context(nc.semaphore(name))

        h = sb(ctx, "h", [P, KT, L])
        x_hi = sb(ctx, "x_hi", [P, KT, L], f32r)
        x_lo = sb(ctx, "x_lo", [P, KT, L], f32r)
        raw = [sb(ctx, f"raw{s}", [P, 8, UC]) for s in range(2)]
        w_hi = [sb(ctx, f"w_hi{s}", [P, 8, UC], f32r) for s in range(2)]
        w_lo = [sb(ctx, f"w_lo{s}", [P, 8, UC], f32r) for s in range(2)]
        cst = sb(ctx, "cst", [P, NCONST])
        ident = cst[:, C_ID:C_ID + P]
        block_mean = cst[:, C_BLK:C_BLK + P]
        all_mean = cst[:, C_ONE:C_ONE + P]
        pool_fix = cst[:, C_CNT:C_CNT + 4 * PAD].rearrange("p (g t) -> p g t", g=4)
        cos, sin = cst[:, C_COS:C_COS + L], cst[:, C_SIN:C_SIN + L]
        rinv = sb(ctx, "rinv", [P, L])
        sumsq = sb(ctx, "sumsq", [P, L])
        sq = sb(ctx, "sq", [P, 2, L])
        q_sin, q_cos = sq[:, 0], sq[:, 1]
        ms_work = sb(ctx, "ms_work", [P, L])
        par_all = sb(ctx, "par_all", [P, DEPTH, NPAR])
        sink_all = sb(ctx, "sink_all", [P, DEPTH, 4])
        par = sb(ctx, "par", [P, NPAR])
        nsink = sb(ctx, "nsink", [P, 4])
        eps = sb(ctx, "eps", [P, 1])

        with ExitStack() as sc:
            q_rot = sb(sc, "q_rot", [P, N_KV_HEADS, NB, 2 * CHUNK])
            k_dup = sb(sc, "k_dup", [P, N_KV_HEADS, L])
            v_T = sb(sc, "v_T", [P, L])
            v_win = sb(sc, "v_win", [P, NWIN, P])
            v_meta = sb(sc, "v_meta", [N_META, P])
            u_sb = sb(sc, "u_sb", [P, 2, PAD + L])
            run_a = sb(sc, "run_a", [P, PAD + L])
            run_b = sb(sc, "run_b", [P, PAD + L])
            pooled = sb(sc, "pooled", [P, 2, L])
            pool_hi = sb(sc, "pool_hi", [P, 2, L], f32r)
            pool_lo = sb(sc, "pool_lo", [P, 2, L], f32r)
            mix_hi = sb(sc, "mix_hi", [P, KT, L], f32r)
            mix_lo = sb(sc, "mix_lo", [P, KT, L], f32r)
            head = sb(sc, "head", [P, 2, L])
            head_sq = sb(sc, "head_sq", [P, NB, 2 * CHUNK])
            q_scale = sb(sc, "q_scale", [P, NB, 2, N_KV_HEADS])
            sine = v_T[:]
            rot_c = sb(sc, "rot_c", [P, L])
            rot_s = sb(sc, "rot_s", [P, L])
            k_win = sb(sc, "k_win", [P, N_KV_HEADS, NWIN, NKEY])
            probs = sb(sc, "probs", [P, 2, 4, NKEY])
            probs_win = sb(sc, "probs_win", [P, 2, 4 * P])
            probs_meta = sb(sc, "probs_meta", [N_META, 2, 4 * P])
            nmax = sb(sc, "nmax", [P, 2, 4])
            nm = sb(sc, "nm", [P, 2, 4])
            sink_arg = sb(sc, "sink_arg", [P, 2, 4])
            sink_exp = sb(sc, "sink_exp", [P, 2, 4])
            row_sum = sb(sc, "row_sum", [P, 2, 4])
            den = sb(sc, "den", [P, 2, 4])
            rden = sb(sc, "rden", [P, 2, 4])
        with ExitStack() as sc:
            m_hi = sb(sc, "m_hi", [P, FT, L], f32r)
            m_lo = sb(sc, "m_lo", [P, FT, L], f32r)
            gate = [sb(sc, f"gate{c}", [P, 2 + L]) for c in range(2)]
            conv = [sb(sc, f"conv{c}", [P, L]) for c in range(2)]
            up = [sb(sc, f"up{c}", [P, L]) for c in range(2)]
            cpar = sb(sc, "cpar", [P, 4, 2])
        with ExitStack() as sc:
            x_in = sb(sc, "x_in", [P, SEQ // P, D_MODEL])
            meta_in = sb(sc, "meta_in", [N_META, D_MODEL])
            par_in = sb(sc, "par_in", [NPAR, DEPTH, P])
            sink_in = sb(sc, "sink_in", [P, DEPTH, 2, 2])
            y_out = sb(sc, "y_out", [P, SEQ // P, D_MODEL])

        slot = [ctx.enter_context(nc.psum_tensor(f"slot{s}", [P, 2, 512], f32)) for s in range(4)]

        side = slot[3][:, 1, 0:HALF]

        def halves(s):
            return slot[s][:, :, 0:HALF]

        def tok(ap):
            return ap.rearrange("p (a t) -> p a t", a=2)

        x_loaded = [sem(f"x_loaded{t}") for t in range(SEQ // P)]
        meta_loaded, const_loaded, par_loaded = sem("meta_loaded"), sem("const_loaded"), sem("par_loaded")
        ident_loaded, sink_loaded = sem("ident_loaded"), sem("sink_loaded")
        raw_loaded = [sem("raw_loaded0"), sem("raw_loaded1")]
        hi_split = [sem("hi_split0"), sem("hi_split1")]
        lo_split = [sem("lo_split0"), sem("lo_split1")]
        down_used = sem("down_used")
        filled = [sem(f"filled{s}") for s in range(5)]
        evac = [sem(f"evac{s}") for s in range(5)]
        eps_ready = sem("eps_ready")
        par_ready = sem("par_ready")
        xhi_ready, xlo_ready = sem("xhi_ready"), sem("xlo_ready")
        sq_ready = sem("sq_ready")
        sq_added = sem("sq_added")
        run_ready = sem("run_ready")
        pooled_ready = sem("pooled_ready")
        phi_ready, plo_ready = sem("phi_ready"), sem("plo_ready")
        headsq_ready = sem("headsq_ready")
        headn_ready = sem("headn_ready")
        qtab_ready = sem("qtab_ready")
        sine_ready = sem("sine_ready")
        rots_ready = sem("rots_ready")
        q_ready = sem("q_ready")
        k_ready = sem("k_ready")
        kwin_ready = sem("kwin_ready")
        nm_ready = sem("nm_ready")
        probs_ready = sem("probs_ready")
        meta_out = sem("meta_out")
        mixhi_ready = sem("mixhi_ready")
        tap2_ready = sem("tap2_ready")
        conv_ready = sem("conv_ready")
        gelu_ready = sem("gelu_ready")
        m_ready = sem("m_ready")
        mhi_ready, mlo_ready = sem("mhi_ready"), sem("mlo_ready")
        dve_par, dve_rot, dve_attn, dve_ffn = sem("dve_par"), sem("dve_rot"), sem("dve_attn"), sem("dve_ffn")
        pool_run, pool_rot, act_log = sem("pool_run"), sem("pool_rot"), sem("act_log")
        y_ready, y_stored = [sem("y_ready0"), sem("y_ready1")], [sem("y_stored0"), sem("y_stored1")]

        MIX_ORDER = ["heads0", "heads1", "heads2", "heads3", "pool0a", "heads4", "pool0b", "pool1a", "heads5",
                     "pool1b", "heads6", "heads7", "pool2", "pool3", "heads8"]

        def mix_count(l, name):
            return l * len(MIX_ORDER) + (MIX_ORDER.index(name) + 1)

        ROTATED = ["q0", "k", "q1", "q2", "q3"]

        def rotated_before(l, n):
            name = ROTATED[n - 1]
            return (k_ready, l + 1) if name == "k" else (q_ready, l * 4 + (int(name[1]) + 1))

        class Chain:
            def __init__(self, eng, semaphore, turn, per):
                self.eng, self.sem, self.base, self.per, self.n = eng, semaphore, turn * per, per, 0

            def link(self, ins):
                self.n += 1
                ins.then_inc(self.sem, 1)
                self.eng.wait_ge(self.sem, self.base + self.n)

            def close(self):
                assert self.n == self.per, (self.n, self.per)

        def slot_turn(l, unit, pairs=0):
            return l * (UNITS // 2) + pairs + unit // 2

        def unit_rows(unit):
            if unit == U_POOL:
                return 2
            if unit >= U_DOWN:
                a, b = DOWN_K[(unit - U_DOWN) % 3]
                return b - a
            return 8

        def last_user_done(l, unit, i=0):
            old = unit - 2
            if old < 0:
                if old + UNITS == UNITS - 1:
                    name = f"down{KT - 1}"
                    return filled[ps.slot(name)], ps.before_last_layer(name, l) + 1
                return down_used, l * KT + 1
            if old >= U_DOWN:
                j, n = divmod(old - U_DOWN, 3)
                if n < 2:
                    return down_used, l * KT + (2 * j + n + 2)
                name = f"down{2 * j + 1}"
            elif old >= U_FFN:
                name = "gate1" if old == U_FFN else "up1"
            elif old >= U_OUT:
                name = f"out{2 * (old - U_OUT) + 1}"
            else:
                name = ("v", "q1", "q3", "u1b", "u3b", "pool3")[old]
            return filled[ps.slot(name)], ps.before(name, l, i) + 1

        def split_hi(act, l, unit, i=0):
            s, t, nk = unit % 2, slot_turn(l, unit, i), unit_rows(unit)
            act.wait_ge(*last_user_done(l, unit, i))
            act.wait_ge(raw_loaded[s], t * 32 + 32)
            nc.scalar.activation(w_hi[s][:, 0:nk], raw[s][:, 0:nk], ACT.Copy).then_inc(hi_split[s], 1)

        def split_lo(dve, l, unit, i=0, half=None):
            s, t, nk = unit % 2, slot_turn(l, unit, i), unit_rows(unit)
            a, b = (0, nk) if half is None else (half * nk // 2, (half + 1) * nk // 2)
            dve.wait_ge(hi_split[s], t + 1)
            ins = nc.vector.tensor_tensor(w_lo[s][:, a:b], raw[s][:, a:b], w_hi[s][:, a:b].bitcast(f32), ALU.subtract)
            if b == nk:
                ins.then_inc(lo_split[s], 1)

        def h_from_layer_before(l, k):
            name = f"down{k}"
            return evac[ps.slot(name)], ps.before_last_layer(name, l) + 1

        def pool_map_parts(mix, g, half, s):
            if half is None:
                return tok(mix[:, 4 + g]), halves(s)
            return mix[:, 4 + g, half * HALF:(half + 1) * HALF], side

        def blocks(weights):
            return weights.rearrange("(k p) c -> p k c", p=P)

        BLOCKS = [(0, N_META), (N_META, N_META + CHUNK)] + [(N_META + c * CHUNK, NKEY) for c in range(1, NCH)]

        block = ctx.enter_context(nc.Block())

        @block.sync
        def _(sp):
            sp.dma_start(cst[:, 0:C_CNT], const[:, 0:C_CNT]).then_inc(ident_loaded, 16)
            for t in range(SEQ // P):
                sp.dma_start(x_in[:, t], x[0, t * P:(t + 1) * P, :]).then_inc(x_loaded[t], 16)

            def load(l, unit, src, i=0):
                s, n = unit % 2, unit_rows(unit)
                parts = [(raw[s][:, a:a + n // 2], src[:, a:a + n // 2]) for a in (n // 2, 0)]
                sp.wait_ge(lo_split[s], slot_turn(l, unit, i) + 1)
                for dst, part in parts:
                    sp.dma_start(dst, part).then_inc(raw_loaded[s], 16)

            sp.wait_ge(par_loaded, 16 * 11)
            with sp.Fori(0, DEPTH) as l:
                win, wo, wd = blocks(w_in[l]), blocks(w_out[l]), blocks(w_down[l])
                wg, wu = blocks(w_gate[l]), blocks(w_up[l])
                load(l, U_KV, win[:, :, ATTN_WIDTH:ATTN_WIDTH + UC])
                for j in range(2):
                    load(l, U_Q + j, win[:, :, j * UC:(j + 1) * UC])
                col_u = ATTN_WIDTH + 2 * KV_WIDTH
                load(l, U_U01, win[:, :, col_u:col_u + UC])
                load(l, U_U23, win[:, :, col_u + UC:col_u + 2 * UC])
                s = U_POOL % 2
                sp.wait_ge(lo_split[s], slot_turn(l, U_POOL) + 1)
                flat = w_pool.rearrange("l g c d -> (l g c) d")
                for g in range(2):
                    rows = flat[bass.ds(l * (4 * P) + g * (2 * P), 2 * P)]
                    sp.dma_start(raw[s][:, g].rearrange("p (g d) -> p g d", g=2),
                                 rows.rearrange("(g c) d -> c g d", g=2)).then_inc(raw_loaded[s], 16)
                for j in range(D_MODEL // UC):
                    load(l, U_OUT + j, wo[:, :, j * UC:(j + 1) * UC])
                with sp.Fori(0, FI) as i:
                    load(l, U_FFN, wg[:, :, bass.ds(i * UC, UC)], i)
                    load(l, U_FFN + 1, wu[:, :, bass.ds(i * UC, UC)], i)
                for j in range(D_MODEL // UC):
                    for n, (a, b) in enumerate(DOWN_K):
                        load(l, U_DOWN + 3 * j + n, wd[:, a:b, j * UC:(j + 1) * UC])
            for t in range(SEQ // P):
                for half in range(2):
                    sp.wait_ge(y_ready[half], t + 1)
                    cols = slice(half * 512, (half + 1) * 512)
                    sp.dma_start(out[0, t * P:(t + 1) * P, cols], y_out[:, t, cols]).then_inc(y_stored[half], 16)
            for half in range(2):
                sp.wait_ge(y_stored[half], 16 * (SEQ // P))

        @block.tensor
        def _(pe):
            def open_slot(name, l, turn=0):
                s = ps.slot(name)
                pe.wait_ge(evac[s], ps.before(name, l, turn))
                return s

            def dense(s, ws, col, rows, a_hi, a_lo, first=True, last=True, ready=None, part=None):
                dst = [(half, slot[s][:, half, 0:HALF]) for half in range(2)] if part is None else [(part, side)]
                for n, (r, k) in enumerate(rows):
                    if ready is not None:
                        ready(k)
                    end = last and n == len(rows) - 1
                    cols = slice(col, col + P)
                    for w, a in ((w_hi, a_hi), (w_hi, a_lo), (w_lo, a_hi)):
                        for half, out_half in dst:
                            ins = nc.tensor.matmul(out_half, w[ws][:, r, cols],
                                                   a[:, k, half * HALF:(half + 1) * HALF],
                                                   start=first and n == 0 and w is w_hi and a is a_hi,
                                                   stop=end and w is w_lo)
                return ins

            def column_mean(name, l, weights, src, semaphore, count):
                s = open_slot(name, l)
                pe.wait_ge(semaphore, count)
                for half in range(2):
                    ins = nc.tensor.matmul(slot[s][:, half, 0:HALF], weights, src[:, half * HALF:(half + 1) * HALF],
                                           start=True, stop=True)
                ins.then_inc(filled[s], 1)

            pe.sem_inc(down_used, 1)
            pe.wait_ge(ident_loaded, 16)
            pe.wait_ge(meta_loaded, 16)
            for k in range(KT):
                s, feat = (2 + k) % 4, slice(k * P, (k + 1) * P)
                if k == 3:
                    pe.wait_ge(par_loaded, 16 * 11)
                    for l in range(DEPTH):
                        ins = nc.tensor.transpose(slot[s][:, l, 0:NPAR], par_in[:, l, :], ident[0:NPAR, 0:NPAR])
                    ins.then_inc(filled[s], 1)
                    pe.wait_ge(evac[s], 1)
                if k >= 4:
                    pe.wait_ge(evac[s], ps.PROLOGUE[s] - 1)
                nc.tensor.transpose(slot[s][:, 0, 0:N_META], meta_in[:, feat], ident[0:N_META, 0:N_META])
                for t in range(SEQ // P):
                    if k == 0:
                        pe.wait_ge(x_loaded[t], 16)
                    dst = slot[s][:, 0, N_META + t * P:N_META + (t + 1) * P] if t < 3 else slot[s][:, 1, 0:P]
                    ins = nc.tensor.transpose(dst, x_in[:, t, feat], ident)
                ins.then_inc(filled[s], 1)

            eight = [(k, k) for k in range(KT)]
            with pe.Fori(0, DEPTH) as l:
                def project(name, unit, ready=None):
                    c = int(name in ("v", "u1", "u3", "q1", "q3"))
                    s = open_slot(name, l)
                    if c == 0:
                        pe.wait_ge(lo_split[unit % 2], slot_turn(l, unit) + 2)
                    dense(s, unit % 2, c * P, eight, x_hi, x_lo, ready=ready).then_inc(filled[s], 1)

                def q_means(kv):
                    s = open_slot(f"qn{kv}", l)
                    pe.wait_ge(headsq_ready, l * 5 + (2 * kv + 3))
                    for b in range(NB):
                        ins = nc.tensor.matmul(slot[s][:, 0, 2 * b:2 * b + 2], head_sq[:, b, :],
                                               cst[:, C_BLK:C_BLK + P:HEAD_DIM], start=True, stop=True)
                    ins.then_inc(filled[s], 1)

                project("k", U_KV, ready=lambda k: pe.wait_ge(xlo_ready, l * (2 * KT) + (k + 1)))
                project("v", U_KV)
                column_mean("attn_norm", l, all_mean, sumsq, sq_added, l * (2 * (KT - 1)) + (KT - 1))
                project("q0", U_Q)
                s = open_slot("v_T", l)
                pe.wait_ge(evac[ps.slot("v")], ps.before("v", l) + 1)
                flat = slot[s][:].rearrange("p a t -> p (a t)")
                for w in range(NWIN):
                    t0 = N_META + w * CHUNK
                    nc.tensor.transpose(flat[:, w * P:(w + 1) * P], v_T[:, t0:t0 + P], ident)
                nc.tensor.transpose(flat[0:N_META, NWIN * P:(NWIN + 1) * P], v_T[:, 0:N_META], ident)\
                  .then_inc(filled[s], 1)
                k_squares = head_sq[:].rearrange("p b q -> p (b q)")[:, 0:L]
                column_mean("k_sq", l, block_mean, k_squares, headsq_ready, l * 5 + 1)
                project("q1", U_Q)
                project("q2", U_Q + 1)
                q_means(0)
                project("q3", U_Q + 1)
                project("u0", U_U01)
                q_means(1)

                def project_side(g, half):
                    name, unit = f"u{g}{'ab'[half]}", U_U01 if g == 1 else U_U23
                    s = open_slot(name, l)
                    if g == 2 and half == 0:
                        pe.wait_ge(lo_split[unit % 2], slot_turn(l, unit) + 2)
                    dense(None, unit % 2, (g % 2) * P, eight, x_hi, x_lo, part=half).then_inc(filled[s], 1)

                def pool_map(g, half=None):
                    name = f"pool{g}" if half is None else f"pool{g}{'ab'[half]}"
                    s = open_slot(name, l)
                    if g == 0 and half == 0:
                        pe.wait_ge(lo_split[U_POOL % 2], slot_turn(l, U_POOL) + 2)
                    pe.wait_ge(plo_ready, l * 4 + (g + 1))
                    dense(s, U_POOL % 2, (g % 2) * P, [(g // 2, g % 2)], pool_hi, pool_lo, part=half)\
                      .then_inc(filled[s], 1)

                def scores(b):
                    q0, nk = BLOCKS[b]
                    s = open_slot(f"scores{b}", l)
                    if b == 0:
                        pe.wait_ge(k_ready, l + 1)
                        pe.wait_ge(q_ready, l * 4 + 4)
                    if b == 2:
                        pe.wait_ge(kwin_ready, l + 1)
                    for t in range(4):
                        j2, kv = divmod(t, 2)
                        part = slice(j2 * HEAD_DIM, (j2 + 1) * HEAD_DIM)
                        keys = k_dup[part, kv, 0:nk] if b < 2 else k_win[part, kv, b - 2, :]
                        ins = nc.tensor.matmul(slot[s][:, j2, kv * nk:(kv + 1) * nk], q_rot[part, kv, b], keys,
                                               start=True, stop=True)
                    ins.then_inc(filled[s], 1)

                def probs_T(b):
                    nk = BLOCKS[b][1]
                    s = open_slot(f"probs_T{b}", l)
                    if b > 1:
                        pe.wait_ge(meta_out, l * (NB - 1) + (b - 1))
                    pe.wait_ge(probs_ready, l * NB + (b + 1))
                    for t in range(4):
                        ins = nc.tensor.transpose(slot[s][0:N_META, 1, t * P:(t + 1) * P],
                                                  probs[:, b % 2, t, 0:N_META], ident)
                        if nk > N_META:
                            ins = nc.tensor.transpose(slot[s][0:nk - N_META, 0, t * P:(t + 1) * P],
                                                      probs[:, b % 2, t, N_META:nk], ident)
                    ins.then_inc(filled[s], 1)

                def heads(b):
                    n = BLOCKS[b][1] - N_META
                    s = open_slot(f"heads{b}", l)
                    name = f"probs_T{b}"
                    pe.wait_ge(evac[ps.slot(name)], ps.before(name, l) + 1)
                    if b > 0:
                        pe.wait_ge(meta_out, l * (NB - 1) + b)
                    for t in range(4):
                        j2, kv = divmod(t, 2)
                        dst = slot[s][j2 * HEAD_DIM:(j2 + 1) * HEAD_DIM, 0, kv * P:(kv + 1) * P]
                        dims, cols = slice(kv * HEAD_DIM, (kv + 1) * HEAD_DIM), slice(t * P, (t + 1) * P)
                        ins = nc.tensor.matmul(dst, v_meta[:, dims], probs_meta[:, b % 2, cols],
                                               start=True, stop=n == 0)
                        if n > 0:
                            ins = nc.tensor.matmul(dst, v_win[0:n, max(b - 2, 0), dims], probs_win[0:n, b % 2, cols],
                                                   start=False, stop=True)
                    ins.then_inc(filled[s], 1)

                name = "heads0"
                pe.wait_ge(evac[ps.slot(name)], ps.before(name, l))
                for step in range(NB + 2):
                    if step < NB:
                        scores(step)
                    if step < 6:
                        project_side(1 + step // 2, step % 2)
                    if step in (6, 7):
                        pool_map(step - 6, 0)
                    if step == NB + 1:
                        pool_map(3)
                    if step >= 2:
                        heads(step - 2)
                    if 1 <= step <= NB:
                        probs_T(step - 1)
                    if step in (6, 7):
                        pool_map(step - 6, 1)
                    if step == NB:
                        pool_map(2)

                rows = [(k, k) for k in (4, 5, 6, 7, 0, 1, 2, 3)]

                def mixed(k):
                    if k == 4:
                        pe.wait_ge(meta_out, l * (NB - 1) + (NB - 1))
                    if k >= 4:
                        name = ("pool0b", "pool1b", "pool2", "pool3")[k - 4]
                        pe.wait_ge(evac[ps.slot(name)], ps.before(name, l) + 1)
                    if k == 0:
                        name = f"heads{NB - 1}"
                        pe.wait_ge(evac[ps.slot(name)], ps.before(name, l) + 1)

                with pe.Fori(0, 2) as i:
                    for t in range(4):
                        s, unit = open_slot(f"out{t}", l, i), U_OUT + t // 2
                        if t % 2 == 0:
                            pe.wait_ge(lo_split[unit % 2], slot_turn(l, unit, i) + 2)
                        dense(s, unit % 2, (t % 2) * P, rows, mix_hi, mix_lo, ready=mixed if t == 0 else None)\
                          .then_inc(filled[s], 1)

                def mlp_tiles(i, ready=None):
                    for n, name in enumerate(("gate0", "gate1", "up0", "up1")):
                        s, unit = open_slot(name, l, i), U_FFN + n // 2
                        if n % 2 == 0:
                            pe.wait_ge(lo_split[unit % 2], slot_turn(l, unit, i) + 2)
                        dense(s, unit % 2, (n % 2) * P, eight, x_hi, x_lo,
                              ready=ready if n == 0 else None).then_inc(filled[s], 1)
                        if n == 0 and ready is not None:
                            column_mean("ffn_norm", l, all_mean, sumsq, sq_added,
                                        l * (2 * (KT - 1)) + 2 * (KT - 1))

                mlp_tiles(0, ready=lambda k: pe.wait_ge(xlo_ready, l * (2 * KT) + (KT + k + 1)))
                with pe.Fori(1, FI) as i:
                    mlp_tiles(i)
                with pe.Fori(0, 2) as i:
                    for j in range(2):
                        for n, (a, b) in enumerate(DOWN_K):
                            unit = U_DOWN + 3 * j + n
                            for c in range(2):
                                name = f"down{2 * j + c}"
                                s = open_slot(name, l, i) if n == 0 else ps.slot(name)
                                if c == 0:
                                    pe.wait_ge(lo_split[unit % 2], slot_turn(l, unit, i * 3) + 2)
                                    pe.wait_ge(mlo_ready, l * FT + b)
                                ins = dense(s, unit % 2, c * P, [(k - a, k) for k in range(a, b)],
                                            m_hi, m_lo, first=n == 0, last=n == 2)
                                if n == 2:
                                    ins.then_inc(filled[s], 1)
                                elif c == 1:
                                    ins.then_inc(down_used, 1)

            for s in range(4):
                pe.wait_ge(evac[s], ps.PROLOGUE[s] + ps.uses[s] * DEPTH)
            for t in range(SEQ // P):
                t0 = N_META + t * P
                for k in range(KT):
                    ins = nc.tensor.transpose(slot[t][:, k // 4, (k % 4) * P:(k % 4 + 1) * P], h[:, k, t0:t0 + P], ident)
                ins.then_inc(filled[t], 1)

        @block.gpsimd
        def _(pool):
            def sum_squares(norm):
                for k in range(1, KT):
                    pool.wait_ge(sq_ready, norm * KT + (k + 1))
                    if k == 1:
                        ins = nc.gpsimd.tensor_tensor(sumsq[:], sq[:, 0], sq[:, 1], ALU.add)
                    else:
                        pool.wait_ge(sq_added, norm * (KT - 1) + (k - 1))
                        ins = nc.gpsimd.tensor_tensor(sumsq[:], sumsq[:], sq[:, k % 2], ALU.add)
                    ins.then_inc(sq_added, 1)

            pool.wait_ge(const_loaded, 16)
            with pool.Fori(0, DEPTH) as l:
                sum_squares(l * 2)
                pads = Chain(pool, pool_run, l, 1)
                nc.gpsimd.memset(u_sb[:, :, 0:PAD], 0.0)
                nc.gpsimd.memset(run_a[:, 0:PAD], 0.0)
                pads.link(nc.gpsimd.memset(run_b[:, 0:PAD], 0.0))
                steps = Chain(pool, pool_rot, l, 10 + 5)

                def rotated(n):
                    name = ROTATED[n]
                    if n > 0:
                        pool.wait_ge(*rotated_before(l, n))
                    if name == "k":
                        pool.wait_ge(headn_ready, l + 1)
                        steps.link(nc.gpsimd.tensor_tensor(rot_c[:], k_dup[:, 0], cos, ALU.mult))
                        pool.wait_ge(rots_ready, l * 5 + (n + 1))
                        for kv in range(N_KV_HEADS):
                            src = slice(kv * HEAD_DIM, (kv + 1) * HEAD_DIM)
                            for half in range(2):
                                ins = nc.gpsimd.tensor_tensor(k_dup[half * HEAD_DIM:(half + 1) * HEAD_DIM, kv],
                                                              rot_c[src], rot_s[src], ALU.add)
                        ins.then_inc(k_ready, 1)
                        return
                    j = int(name[1])
                    pool.wait_ge(evac[ps.slot(name)], ps.before(name, l) + 1)
                    pool.wait_ge(qtab_ready, l + 1)
                    steps.link(nc.gpsimd.tensor_tensor(rot_c[:], head[:, j % 2], q_cos, ALU.mult))
                    pool.wait_ge(rots_ready, l * 5 + (n + 1))
                    kv, cols = j // 2, slice(j % 2 * CHUNK, (j % 2 + 1) * CHUNK)
                    chunks = [r[:, N_META:].rearrange("p (b q) -> p b q", q=CHUNK) for r in (rot_c, rot_s)]
                    nc.gpsimd.tensor_tensor(q_rot[:, kv, 0, cols], rot_c[:, 0:CHUNK], rot_s[:, 0:CHUNK], ALU.add)
                    nc.gpsimd.tensor_tensor(q_rot[:, kv, 1:, cols], *chunks, ALU.add).then_inc(q_ready, 1)

                def group(g):
                    name = f"u{g}b" if g else "u0"
                    pool.wait_ge(evac[ps.slot(name)], ps.before(name, l) + 1)
                    if g > 0:
                        pool.wait_ge(pooled_ready, l * 4 + g)
                    src, step = u_sb[:, g % 2], 1
                    for n in range(g + 1):
                        dst = (run_a, run_b)[(n + g) % 2]
                        steps.link(nc.gpsimd.tensor_tensor(dst[:, PAD:], src[:, PAD:],
                                                           src[:, PAD - step:PAD + L - step], ALU.add))
                        src, step = dst[:, :], step * 2
                    nc.gpsimd.tensor_tensor(run_a[:, PAD:2 * PAD], run_a[:, PAD:2 * PAD], pool_fix[:, g],
                                            ALU.mult).then_inc(run_ready, 1)

                for n in range(5):
                    rotated(n)
                for g in range(4):
                    group(g)
                steps.close()
                sum_squares(l * 2 + 1)
                with pool.Fori(0, FI) as i:
                    for c in range(2):
                        u = ps.slot(f"up{c}")
                        pool.wait_ge(gelu_ready, l * FT + i * 2 + (c + 1))
                        pool.wait_ge(evac[u], ps.before(f"up{c}", l, i) + 1)
                        nc.gpsimd.tensor_tensor(up[c][:], up[c][:], conv[c][:], ALU.mult).then_inc(m_ready, 1)

        @block.scalar
        def _(act):
            act.dma_start(meta_in[:], meta_tokens).then_inc(meta_loaded, 16)
            by_row = "l (r p) -> r l p"
            for src, r, n in ((attn_norm_g, R_AG, KT), (ffn_norm_g, R_FG, KT), (pool_scale, R_PS, 4),
                              (conv_b, R_CB, FT), (conv_w[:, 0], R_CW, FT), (conv_w[:, 1], R_CW + FT, FT),
                              (conv_w[:, 2], R_CW + 2 * FT, FT)):
                act.dma_start(par_in[r:r + n], src.rearrange(by_row, p=P)).then_inc(par_loaded, 16)
            for src, r in ((q_norm_g, R_QG), (k_norm_g, R_KG)):
                for half in range(2):
                    act.dma_start(par_in[r:r + 1, :, half * HEAD_DIM:(half + 1) * HEAD_DIM],
                                  src.rearrange("(a l) d -> a l d", a=1)).then_inc(par_loaded, 16)
            for l in range(DEPTH):
                for jp in range(2):
                    act.dma_start(sink_in[jp * 64:(jp + 1) * 64, l],
                                  sinks[l].rearrange("(kv jp j) -> jp kv j", jp=2, j=2)[jp]
                                  .partition_broadcast(64)).then_inc(sink_loaded, 16)
            act.dma_start(cst[:, C_CNT:], const[:, C_CNT:]).then_inc(const_loaded, 16)

            def gain_hi(k, ready, row):
                act.wait_ge(*ready)
                nc.scalar.activation(x_hi[:, k], h[:, k], ACT.Copy, scale=par[:, row + k:row + k + 1])\
                  .then_inc(xhi_ready, 1)

            act.wait_ge(eps_ready, 1)
            with act.Fori(0, DEPTH) as l:
                roots = Chain(act, act_log, l, 2)

                def square(norm, k):
                    if k >= 2:
                        act.wait_ge(sq_added, (l * 2 + norm) * (KT - 1) + max(1, k - 2))
                    nc.scalar.activation(sq[:, k % 2], h[:, k], ACT.Square).then_inc(sq_ready, 1)

                def root(name, dst):
                    s = ps.slot(name)
                    act.wait_ge(filled[s], ps.before(name, l) + 1)
                    roots.link(nc.scalar.activation(tok(ms_work[:]), halves(s), ACT.Ln, bias=eps[:]))
                    nc.scalar.activation(dst, ms_work[:], ACT.Exp, scale=-0.5).then_inc(evac[s], 1)

                def q_squares(j):
                    name = f"q{j}"
                    act.wait_ge(evac[ps.slot(name)], ps.before(name, l) + 1)
                    if j == 2:
                        act.wait_ge(filled[ps.slot("qn0")], ps.before("qn0", l) + 1)
                    cols = slice(j % 2 * CHUNK, (j % 2 + 1) * CHUNK)
                    nc.scalar.activation(head_sq[:, 0, cols], head[:, j % 2, 0:CHUNK], ACT.Square)
                    nc.scalar.activation(head_sq[:, 1:, cols],
                                         head[:, j % 2, N_META:].rearrange("p (b q) -> p b q", q=CHUNK), ACT.Square)\
                      .then_inc(headsq_ready, 1)

                def q_rms(kv):
                    s = ps.slot(f"qn{kv}")
                    act.wait_ge(filled[s], ps.before(f"qn{kv}", l) + 1)
                    nc.scalar.activation(q_scale[:, :, :, kv], slot[s][:, 0, 0:2 * NB].rearrange("p (b j) -> p b j", j=2),
                                         ACT.Sqrt, bias=eps[:]).then_inc(evac[s], 1)

                def shift(n):
                    act.wait_ge(sine_ready, l * 5 + (n + 1))
                    if n > 0:
                        act.wait_ge(*rotated_before(l, n))
                    for to, fr in ((0, 32), (32, 0), (64, 96), (96, 64)):
                        ins = nc.scalar.activation(rot_s[to:to + 32], sine[fr:fr + 32], ACT.Copy)
                    ins.then_inc(rots_ready, 1)

                def pooled_hi(g):
                    act.wait_ge(pooled_ready, l * 4 + (g + 1))
                    if g >= 2:
                        name = f"pool{g - 2}b"
                        act.wait_ge(filled[ps.slot(name)], ps.before(name, l) + 1)
                    nc.scalar.activation(pool_hi[:, g % 2], pooled[:, g % 2], ACT.Copy).then_inc(phi_ready, 1)

                def pool_map_hi(g, half=None):
                    name = f"pool{g}" if half is None else f"pool{g}{'ab'[half]}"
                    s = ps.slot(name)
                    act.wait_ge(filled[s], ps.before(name, l) + 1)
                    dst, src = pool_map_parts(mix_hi, g, half, s)
                    nc.scalar.activation(dst, src, ACT.Copy, scale=par[:, R_PS + g:R_PS + g + 1]).then_inc(mixhi_ready, 1)

                split_hi(act, l, 0)
                act.wait_ge(par_ready, l * 2 + 2)
                for k in range(KT):
                    gain_hi(k, h_from_layer_before(l, k), R_AG)
                for k in range(KT):
                    square(0, k)
                split_hi(act, l, 1)
                split_hi(act, l, 2)
                root("attn_norm", rinv[:])
                act.wait_ge(evac[ps.slot("k")], ps.before("k", l) + 1)
                nc.scalar.activation(head_sq[:].rearrange("p b q -> p (b q)")[:, 0:L], k_dup[:, 0], ACT.Square)\
                  .then_inc(headsq_ready, 1)
                nc.scalar.activation(q_sin, sin, ACT.Copy, scale=par[:, R_QG:R_QG + 1])
                nc.scalar.activation(q_cos, cos, ACT.Copy, scale=par[:, R_QG:R_QG + 1]).then_inc(qtab_ready, 1)
                s = ps.slot("v_T")
                act.wait_ge(filled[s], ps.before("v_T", l) + 1)
                flat = slot[s][:].rearrange("p a t -> p (a t)")
                nc.scalar.activation(v_meta[:], flat[0:N_META, NWIN * P:(NWIN + 1) * P], ACT.Copy)
                nc.scalar.activation(v_win[:, 0:4].rearrange("p w d -> p (w d)"), flat[:, 0:4 * P], ACT.Copy)
                nc.scalar.activation(v_win[:, 4:NWIN].rearrange("p w d -> p (w d)"), flat[:, 4 * P:NWIN * P],
                                     ACT.Copy).then_inc(evac[s], 1)
                s = ps.slot("k_sq")
                act.wait_ge(filled[s], ps.before("k_sq", l) + 1)
                nc.scalar.activation(tok(ms_work[:]), halves(s), ACT.Sqrt, bias=eps[:]).then_inc(evac[s], 1)
                q_squares(0)
                shift(0)
                shift(1)
                q_squares(1)
                split_hi(act, l, 3)
                shift(2)
                act.wait_ge(k_ready, l + 1)
                for kv in range(N_KV_HEADS):
                    nc.scalar.activation(k_win[:, kv, :, 0:N_META],
                                         k_dup[:, kv, 0:N_META].unsqueeze(1).broadcast_to([P, NWIN, N_META]), ACT.Copy)
                    keys = k_dup[:, kv, N_META:]
                    windows = bass.AP(keys.tensor, keys.offset, [list(keys.ap[0]), [CHUNK, NWIN], [1, 2 * CHUNK]])
                    ins = nc.scalar.activation(k_win[:, kv, :, N_META:], windows, ACT.Copy)
                ins.then_inc(kwin_ready, 1)
                q_squares(2)
                shift(3)
                q_rms(0)
                q_squares(3)
                shift(4)
                split_hi(act, l, 4)
                q_rms(1)

                def exps(b):
                    nk, s, y = BLOCKS[b][1], ps.slot(f"scores{b}"), b % 2
                    act.wait_ge(nm_ready, l * NB + b + 1)
                    if b >= 2:
                        old = f"probs_T{b - 2}"
                        act.wait_ge(filled[ps.slot(old)], ps.before(old, l) + 1)
                    nc.scalar.activation(sink_exp[:, y], sink_arg[:, y], ACT.Exp)
                    for t in range(4):
                        col = slice((t % 2) * nk, (t % 2 + 1) * nk)
                        ins = nc.scalar.activation(probs[:, y, t, 0:nk], slot[s][:, t // 2, col], ACT.Exp,
                                                   bias=nm[:, y, t:t + 1],
                                                   scale=q_scale[:, b, t // 2, t % 2:t % 2 + 1], accum_out=row_sum[:, y, t:t + 1])
                    ins.then_inc(evac[s], 1)

                def probs_out(b):
                    n = BLOCKS[b][1] - N_META
                    pt = ps.slot(f"probs_T{b}")
                    act.wait_ge(filled[pt], ps.before(f"probs_T{b}", l) + 1)
                    if n > 0:
                        ins = nc.scalar.activation(probs_win[0:n, b % 2], slot[pt][0:n, 0, :], ACT.Copy)
                    else:
                        ins = nc.scalar.activation(probs_meta[:, 0], slot[pt][0:N_META, 1, :], ACT.Copy)
                    ins.then_inc(evac[pt], 1)

                def heads_hi(b):
                    t0, nq = BLOCKS[b][0], CHUNK if b else N_META
                    hd = ps.slot(f"heads{b}")
                    act.wait_ge(filled[hd], ps.before(f"heads{b}", l) + 1)
                    src = slot[hd][:, 0, 0:4 * CHUNK].rearrange("p (t q) -> p t q", t=4)[:, :, 0:nq]
                    nc.scalar.activation(mix_hi[:, 0:4, t0:t0 + nq], src, ACT.Copy).then_inc(mixhi_ready, 1)

                for step in range(NB + 3):
                    if step >= 3:
                        heads_hi(step - 3)
                    if 2 <= step < NB + 2:
                        probs_out(step - 2)
                    if step in (7, 8):
                        pool_map_hi(step - 7, 1)
                    if step < NB:
                        exps(step)
                    if step in (6, 7):
                        pool_map_hi(step - 6, 0)
                    if step == NB + 1:
                        pool_map_hi(2)
                        pool_map_hi(3)
                    if step == 2:
                        split_hi(act, l, U_POOL)
                    if step == 6:
                        split_hi(act, l, U_OUT)
                    if step in (1, 4, 7, 8):
                        pooled_hi((1, 4, 7, 8).index(step))
                split_hi(act, l, U_OUT + 1)

                for j in range(4):
                    if j < 3:
                        split_hi(act, l, U_OUT + 2 + j)
                    for k in (2 * j, 2 * j + 1):
                        gain_hi(k, (evac[ps.slot(f"out{k}")], ps.before(f"out{k}", l) + 1), R_FG)
                        square(1, k)
                split_hi(act, l, U_OUT + 5)
                root("ffn_norm", rinv[:])
                roots.close()

                with act.Fori(0, FI) as i:
                    for c in range(2):
                        g = ps.slot(f"gate{c}")
                        act.wait_ge(evac[g], ps.before(f"gate{c}", l, i) + 1)
                        nc.scalar.activation(conv[c][:], gate[c][:, 2:], ACT.Identity, bias=cpar[:, 3, c:c + 1],
                                             scale=cpar[:, 2, c:c + 1]).then_inc(tap2_ready, 1)
                    split_hi(act, l, U_FFN + 2, i)
                    for c in range(2):
                        act.wait_ge(conv_ready, l * FT + i * 2 + (c + 1))
                        nc.scalar.activation(conv[c][:], conv[c][:], ACT.Gelu).then_inc(gelu_ready, 1)
                    split_hi(act, l, U_FFN + 3, i)
                    for c in range(2):
                        act.wait_ge(m_ready, l * FT + i * 2 + (c + 1))
                        nc.scalar.activation(m_hi[:, bass.ds(i * 2 + c, 1)].rearrange("p a t -> p (a t)"),
                                             up[c][:], ACT.Copy).then_inc(mhi_ready, 1)
                for unit in range(U_DOWN + 2, UNITS):
                    split_hi(act, l, unit)

            for t in range(SEQ // P):
                act.wait_ge(filled[t], ps.PROLOGUE[t] + ps.uses[t] * DEPTH + 1)
                nc.scalar.activation(y_out[:, t, 0:512], slot[t][:, 0, :], ACT.Copy).then_inc(y_ready[0], 1)

        @block.vector
        def _(dve):
            for s in range(2):
                dve.sem_inc(lo_split[s], 1)
            nc.vector.memset(eps[:], EPS).then_inc(eps_ready, 1)
            for k in range(KT):
                s, cut = (2 + k) % 4, N_META + 3 * P
                if k == 3:
                    dve.wait_ge(filled[s], 1)
                    nc.vector.tensor_copy(par_all[:], slot[s][:, :, 0:NPAR]).then_inc(evac[s], 1)
                dve.wait_ge(filled[s], ps.PROLOGUE[s] - (k < 4))
                nc.vector.tensor_copy(h[:, k, 0:cut], slot[s][:, 0, 0:cut])
                nc.vector.tensor_copy(h[:, k, cut:L], slot[s][:, 1, 0:P]).then_inc(evac[s], 1)
            dve.wait_ge(evac[1], 1)
            dve.wait_ge(sink_loaded, 16 * 2 * DEPTH)
            prep = Chain(dve, dve_par, 0, 2)
            prep.link(nc.vector.tensor_scalar(sink_all[:].rearrange("p l (j kv) -> p l j kv", j=2),
                                              sink_in[:].rearrange("p l kv j -> p l j kv"), -1.0, None, ALU.mult))
            prep.link(nc.vector.tensor_scalar(par_all[:, :, R_QG:R_QG + 1], par_all[:, :, R_QG:R_QG + 1],
                                              float(HEAD_DIM) ** -0.5, None, ALU.mult))
            prep.close()
            dve.wait_ge(const_loaded, 16)

            def gain_lo(k, count, row):
                dve.wait_ge(xhi_ready, count)
                nc.vector.scalar_tensor_tensor(x_lo[:, k], h[:, k], par[:, row + k:row + k + 1],
                                               x_hi[:, k].bitcast(f32), ALU.mult, ALU.subtract)\
                  .then_inc(xlo_ready, 1)

            with dve.Fori(0, DEPTH) as l:
                nc.vector.tensor_copy(par[:], par_all[:, bass.ds(l, 1)].rearrange("p a r -> p (a r)"))\
                  .then_inc(par_ready, 1)
                nc.vector.tensor_copy(nsink[:], sink_all[:, bass.ds(l, 1)].rearrange("p a r -> p (a r)"))\
                  .then_inc(par_ready, 1)
                split_lo(dve, l, 0)
                dve.wait_ge(par_ready, l * 2 + 2)
                for k in range(KT):
                    gain_lo(k, l * (2 * KT) + (k + 1), R_AG)
                split_lo(dve, l, 1)
                split_lo(dve, l, 2)

                def inverse_rms_ready(name):
                    dve.wait_ge(evac[ps.slot(name)], ps.before(name, l) + 1)

                def scaled(name, dst, turn=0):
                    s = ps.slot(name)
                    dve.wait_ge(filled[s], ps.before(name, l, turn) + 1)
                    nc.vector.tensor_tensor(tok(dst), halves(s), tok(rinv[:]), ALU.mult).then_inc(evac[s], 1)

                def q_tile(j):
                    if j >= 2:
                        dve.wait_ge(q_ready, l * 4 + (j - 1))
                    scaled(f"q{j}", head[:, j % 2])

                rot = Chain(dve, dve_rot, l, 2)

                def sine_part(n):
                    name = ROTATED[n]
                    if n > 0:
                        dve.wait_ge(rots_ready, l * 5 + n)
                    if name == "k":
                        dve.wait_ge(headn_ready, l + 1)
                        nc.vector.tensor_tensor(sine, k_dup[:, 0], sin, ALU.mult).then_inc(sine_ready, 1)
                        return
                    dve.wait_ge(evac[ps.slot(name)], ps.before(name, l) + 1)
                    nc.vector.tensor_tensor(sine, head[:, int(name[1]) % 2], q_sin, ALU.mult).then_inc(sine_ready, 1)

                def pooled_tile(g):
                    dve.wait_ge(run_ready, l * 4 + (g + 1))
                    if g >= 2:
                        dve.wait_ge(plo_ready, l * 4 + (g - 1))
                    nc.vector.scalar_tensor_tensor(pooled[:, g % 2], run_a[:, PAD:], 1.0 / POOL_SIZES[g],
                                                   u_sb[:, g % 2, PAD:], ALU.mult, ALU.subtract)\
                      .then_inc(pooled_ready, 1)

                def pooled_lo(g):
                    dve.wait_ge(phi_ready, l * 4 + (g + 1))
                    nc.vector.tensor_tensor(pool_lo[:, g % 2], pooled[:, g % 2], pool_hi[:, g % 2].bitcast(f32),
                                            ALU.subtract).then_inc(plo_ready, 1)

                inverse_rms_ready("attn_norm")
                scaled("k", k_dup[:, 0])
                scaled("v", v_T[:])
                q_tile(0)
                dve.wait_ge(qtab_ready, l + 1)
                dve.wait_ge(evac[ps.slot("v_T")], ps.before("v_T", l) + 1)
                sine_part(0)
                dve.wait_ge(evac[ps.slot("k_sq")], ps.before("k_sq", l) + 1)
                rot.link(nc.vector.reciprocal(ms_work[:], ms_work[:]))
                nc.vector.scalar_tensor_tensor(k_dup[:, 0], k_dup[:, 0], par[:, R_KG:R_KG + 1], ms_work[:],
                                               ALU.mult, ALU.mult).then_inc(headn_ready, 1)
                sine_part(1)
                q_tile(1)
                sine_part(2)
                split_lo(dve, l, 3)
                for j in (2, 3):
                    q_tile(j)
                    sine_part(j + 1)
                split_lo(dve, l, 4)
                scaled("u0", u_sb[:, 0, PAD:])
                for kv in range(2):
                    dve.wait_ge(evac[ps.slot(f"qn{kv}")], ps.before(f"qn{kv}", l) + 1)
                rot.link(nc.vector.reciprocal(q_scale[:], q_scale[:]))
                rot.close()

                def u_half(g, half):
                    name, h0 = f"u{g}{'ab'[half]}", half * HALF
                    if g >= 2 and half == 0:
                        dve.wait_ge(pooled_ready, l * 4 + (g - 1))
                    dve.wait_ge(filled[4], ps.before(name, l) + 1)
                    nc.vector.tensor_tensor(u_sb[:, g % 2, PAD + h0:PAD + h0 + HALF], side, rinv[:, h0:h0 + HALF],
                                            ALU.mult).then_inc(evac[4], 1)

                def pool_map_lo(g, half=None):
                    name = f"pool{g}" if half is None else f"pool{g}{'ab'[half]}"
                    s = ps.slot(name)
                    dve.wait_ge(mixhi_ready, mix_count(l, name))
                    dst, src = pool_map_parts(mix_lo, g, half, s)
                    high = pool_map_parts(mix_hi, g, half, s)[0]
                    nc.vector.scalar_tensor_tensor(dst, src, par[:, R_PS + g:R_PS + g + 1], high.bitcast(f32),
                                                   ALU.mult, ALU.subtract).then_inc(evac[s], 1)

                ch = Chain(dve, dve_attn, l, 5 * NB)

                def row_maxima(b):
                    nk, s, y = BLOCKS[b][1], ps.slot(f"scores{b}"), b % 2
                    dve.wait_ge(filled[s], ps.before(f"scores{b}", l) + 1)
                    view = slot[s][:, :, 0:2 * nk].rearrange("p a (t k) -> p a t k", t=2)
                    ch.link(nc.vector.tensor_reduce(nmax[:, y].rearrange("p (a t) -> p a t", a=2), view, op=ALU.max,
                                                    axis=AX.X, negate=True))
                    ch.link(nc.vector.tensor_tensor(nmax[:, y], nmax[:, y],
                                                    q_scale[:, b].rearrange("p j kv -> p (j kv)"), ALU.mult))
                    ch.link(nc.vector.tensor_tensor(nm[:, y], nmax[:, y], nsink[:], ALU.min))
                    nc.vector.tensor_tensor(sink_arg[:, y], nm[:, y], nsink[:], ALU.subtract).then_inc(nm_ready, 1)

                def divide(b):
                    nk, s, y = BLOCKS[b][1], ps.slot(f"scores{b}"), b % 2
                    dve.wait_ge(evac[s], ps.before(f"scores{b}", l) + 1)
                    ch.link(nc.vector.tensor_tensor(den[:, y], row_sum[:, y], sink_exp[:, y], ALU.add))
                    ch.link(nc.vector.reciprocal(rden[:, y], den[:, y]))
                    nc.vector.tensor_tensor(probs[:, y, :, 0:nk], probs[:, y, :, 0:nk],
                                            rden[:, y].unsqueeze(2).broadcast_to([P, 4, nk]), ALU.mult)\
                      .then_inc(probs_ready, 1)

                def meta_probs_out(b):
                    pt = ps.slot(f"probs_T{b}")
                    dve.wait_ge(filled[pt], ps.before(f"probs_T{b}", l) + 1)
                    nc.vector.tensor_copy(probs_meta[:, b % 2], slot[pt][0:N_META, 1, :]).then_inc(meta_out, 1)

                def heads_lo(b):
                    t0, nq = BLOCKS[b][0], CHUNK if b else N_META
                    hd = ps.slot(f"heads{b}")
                    dve.wait_ge(mixhi_ready, mix_count(l, f"heads{b}"))
                    src = slot[hd][:, 0, 0:4 * CHUNK].rearrange("p (t q) -> p t q", t=4)[:, :, 0:nq]
                    nc.vector.tensor_tensor(mix_lo[:, 0:4, t0:t0 + nq], src,
                                            mix_hi[:, 0:4, t0:t0 + nq].bitcast(f32), ALU.subtract)\
                      .then_inc(evac[hd], 1)

                for step in range(NB + 3):
                    if 3 <= step < NB + 2:
                        meta_probs_out(step - 2)
                    if step >= 3:
                        heads_lo(step - 3)
                    if step in (7, 8):
                        pool_map_lo(step - 7, 1)
                    if step < NB:
                        row_maxima(step)
                    if 1 <= step <= NB:
                        divide(step - 1)
                    if step < 6:
                        u_half(1 + step // 2, step % 2)
                    if step in (6, 7):
                        pool_map_lo(step - 6, 0)
                    if step == NB + 1:
                        pool_map_lo(2)
                        pool_map_lo(3)
                    if step in (0, 3, 6, 7):
                        pooled_tile((0, 3, 6, 7).index(step))
                    if step in (2, 5, 8, 9):
                        pooled_lo((2, 5, 8, 9).index(step))
                    if step == 3:
                        split_lo(dve, l, U_POOL)
                    if step in (7, 8):
                        split_lo(dve, l, U_OUT, half=step - 7)
                ch.close()
                split_lo(dve, l, U_OUT + 1)

                def add_to_h(name, k):
                    s = ps.slot(name)
                    dve.wait_ge(filled[s], ps.before(name, l) + 1)
                    nc.vector.tensor_tensor(tok(h[:, k]), halves(s), tok(h[:, k]), ALU.add).then_inc(evac[s], 1)

                for j in range(4):
                    for k in (2 * j, 2 * j + 1):
                        add_to_h(f"out{k}", k)
                    if j < 3:
                        split_lo(dve, l, U_OUT + 2 + j)
                    for k in (2 * j, 2 * j + 1):
                        gain_lo(k, l * (2 * KT) + (KT + k + 1), R_FG)
                split_lo(dve, l, U_OUT + 5)

                inverse_rms_ready("ffn_norm")
                for c in range(2):
                    nc.vector.memset(gate[c][:, 0:2], 0.0)
                taps = par[:, R_CW:R_CW + 4 * FT].rearrange("p (t f) -> p t f", t=4)
                with dve.Fori(0, FI) as i:
                    ch = Chain(dve, dve_ffn, l * FI + i, 3)
                    ch.link(nc.vector.tensor_copy(cpar[:], taps[:, :, bass.ds(i * 2, 2)]))
                    for c in range(2):
                        scaled(f"gate{c}", gate[c][:, 2:], i)
                    split_lo(dve, l, U_FFN + 2, i)
                    for c in range(2):
                        dve.wait_ge(tap2_ready, l * FT + i * 2 + (c + 1))
                        ch.link(nc.vector.scalar_tensor_tensor(conv[c][:], gate[c][:, 1:1 + L], cpar[:, 1, c:c + 1],
                                                               conv[c][:], ALU.mult, ALU.add))
                        nc.vector.scalar_tensor_tensor(conv[c][:], gate[c][:, 0:L], cpar[:, 0, c:c + 1],
                                                       conv[c][:], ALU.mult, ALU.add).then_inc(conv_ready, 1)
                    ch.close()
                    for c in range(2):
                        scaled(f"up{c}", up[c][:], i)
                    split_lo(dve, l, U_FFN + 3, i)
                    for c in range(2):
                        dve.wait_ge(mhi_ready, l * FT + i * 2 + (c + 1))
                        one = bass.ds(i * 2 + c, 1)
                        nc.vector.tensor_tensor(m_lo[:, one].rearrange("p a t -> p (a t)"), up[c][:],
                                                m_hi[:, one].rearrange("p a t -> p (a t)").bitcast(f32),
                                                ALU.subtract).then_inc(mlo_ready, 1)
                for j in range(4):
                    for n in range(3):
                        unit = U_DOWN + 3 * j + n
                        if n == 2:
                            for k in (2 * j, 2 * j + 1):
                                add_to_h(f"down{k}", k)
                        if unit + 2 < UNITS:
                            split_lo(dve, l, unit + 2)

            for t in range(SEQ // P):
                dve.wait_ge(filled[t], ps.PROLOGUE[t] + ps.uses[t] * DEPTH + 1)
                nc.vector.tensor_copy(y_out[:, t, 512:], slot[t][:, 1, :]).then_inc(y_ready[1], 1)


def constant_table():
    import numpy as np

    table = np.zeros((P, NCONST), np.float32)
    table[:, C_ID:C_ID + P] = np.eye(P, dtype=np.float32)
    heads = np.arange(P) // HEAD_DIM
    table[:, C_BLK:C_BLK + P] = (heads[:, None] == heads[None, :]).astype(np.float32) / HEAD_DIM
    table[:, C_ONE:C_ONE + P] = 1.0 / D_MODEL
    t = np.arange(PAD)
    for g, w in enumerate(POOL_SIZES):
        table[:, C_CNT + g * PAD:C_CNT + (g + 1) * PAD] = w / np.minimum(t + 1, w)
    half = HEAD_DIM // 2
    inv = (1.0 / (np.float32(ROPE_THETA) ** (np.arange(0, HEAD_DIM, 2, dtype=np.float32) / np.float32(HEAD_DIM))))
    angle = np.arange(L, dtype=np.float32)[None, :] * inv.astype(np.float32)[:, None]
    feature = np.arange(P) % half
    sign = np.where(np.arange(P) % HEAD_DIM < half, 1.0, -1.0).astype(np.float32)
    table[:, C_COS:C_COS + L] = np.cos(angle)[feature]
    table[:, C_SIN:C_SIN + L] = np.sin(angle)[feature] * sign[:, None]
    return table


_INS = ["x", "meta_tokens", "attn_norm_g", "w_in", "q_norm_g", "k_norm_g", "sinks", "w_pool", "pool_scale",
        "w_out", "ffn_norm_g", "w_gate", "w_up", "conv_w", "conv_b", "w_down"]


def kernel(**inputs):
    import numpy as _np
    import concourse.bacc as _bacc
    from concourse.bass_utils import run_bass_kernel_spmd as _run

    nc = _bacc.Bacc("TRN2", target_bir_lowering=False, num_devices=1, dynamic_dma_scratch_size=256)
    arrays, args = {}, []
    for name in _INS:
        a = _np.ascontiguousarray(inputs[name])
        arrays[f"in_{name}"] = a
        args.append(nc.dram_tensor(f"in_{name}", a.shape, mybir.dt.from_np(a.dtype), kind="ExternalInput").ap())
    table = constant_table()
    arrays["const_table"] = table
    args.append(nc.dram_tensor("const_table", table.shape, mybir.dt.float32, kind="ExternalInput").ap())
    args.append(nc.dram_tensor("out", (1, SEQ, D_MODEL), mybir.dt.float32, kind="ExternalOutput").ap())
    build_trunk(nc, *args)
    result = _run(nc, [arrays], core_ids=[0])
    return result.results[0]["out"]
```

```python
import concourse.bass as bass
from concourse import mybir
from contextlib import ExitStack

D_MODEL, SEQ, DEPTH = 1024, 512, 2
CHUNK, N_META, HEAD_DIM = 64, 16, 64
N_Q_HEADS, N_KV_HEADS = 8, 2
ATTN_WIDTH = N_Q_HEADS * HEAD_DIM
KV_WIDTH = N_KV_HEADS * HEAD_DIM
POOL_WIDTH = D_MODEL - ATTN_WIDTH
POOL_SIZES = (2, 4, 8, 16)
IN_WIDTH = ATTN_WIDTH + 2 * KV_WIDTH + POOL_WIDTH
D_FF = ((8 * D_MODEL // 3 + 127) // 128) * 128
EPS = 1e-6
ROPE_THETA = 10000.0

P = 128
L = N_META + SEQ
HALF = L // 2
KT = D_MODEL // P
FT = D_FF // P
FI = FT // 2
UC = 2 * P
PAD = max(POOL_SIZES)
NCH = SEQ // CHUNK
NB = NCH + 1
NKEY = N_META + 2 * CHUNK
NWIN = NCH - 1

U_KV, U_Q, U_U23, U_U01, U_POOL, U_OUT = 0, 1, 3, 4, 5, 6
U_FFN = U_OUT + D_MODEL // UC
U_DOWN = U_FFN + 2 * FI
DOWN_K = [(0, 8), (8, 16), (16, FT)]
UNITS = U_DOWN + len(DOWN_K) * (D_MODEL // UC)

R_AG, R_FG, R_PS, R_CW = 0, KT, 2 * KT, 2 * KT + 4
R_CB = R_CW + 3 * FT
R_QG, R_KG = R_CB + FT, R_CB + FT + 1
NPAR = R_KG + 1

C_ID, C_BLK, C_ONE, C_CNT, C_COS, C_SIN = 0, P, 2 * P, 3 * P, 3 * P + 4 * PAD, 3 * P + 4 * PAD + L
NCONST = C_SIN + L


class Psum:
    PROLOGUE = [2, 3, 2, 2, 1]

    def __init__(self):
        self.at, self.uses = {}, [0, 0, 0, 0, 0]
        order = [("k", 2), ("v", 3), ("attn_norm", 0), ("q0", 1), ("v_T", 0), ("k_sq", 3), ("q1", 2),
                 ("q2", 1), ("qn0", 0), ("q3", 3), ("u3", 2), ("qn1", 0)]
        for b in range(NB):
            order += [(f"scores{b}", 1 - b % 2)] + {5: [("pool3", 1)], 8: [("pool2", 0), ("pool1", 0)]}.get(b, [])
        order += [("pool0", 1)] + [(f"{kind}{b}", s) for b in range(NB) for kind, s in (("probs_T", 2), ("heads", 3))]
        order += [(f"u{g}{half}", 4) for g in (2, 1, 0) for half in "ab"]
        order += [(f"out{t}", (2 + t) % 4) for t in range(KT)] + [("ffn_norm", 0)]
        order += [("gate0", 2), ("gate1", 3), ("up0", 0), ("up1", 1)] * FI
        order += [(f"down{t}", (2 + t) % 4) for t in range(KT)]
        for name, slot in order:
            self.at.setdefault(name, (slot, self.uses[slot]))
            self.uses[slot] += 1

    def slot(self, name):
        return self.at[name][0]

    def before(self, name, layer, turn=0):
        slot, n = self.at[name]
        return layer * self.uses[slot] + turn + (self.PROLOGUE[slot] + n)

    def before_last_layer(self, name, layer):
        slot, n = self.at[name]
        return layer * self.uses[slot] + (self.PROLOGUE[slot] + n - self.uses[slot])


def build_trunk(nc, x, meta_tokens, attn_norm_g, w_in, q_norm_g, k_norm_g, sinks, w_pool, pool_scale,
                w_out, ffn_norm_g, w_gate, w_up, conv_w, conv_b, w_down, const, out):
    f32, f32r = mybir.dt.float32, mybir.dt.float32r
    ALU, ACT, AX = mybir.AluOpType, mybir.ActivationFunctionType, mybir.AxisListType
    ps = Psum()

    with ExitStack() as ctx:
        def sb(stack, name, shape, dt=f32):
            return stack.enter_context(nc.sbuf_tensor(name, shape, dt))

        def sem(name):
            return ctx.enter_context(nc.semaphore(name))

        h = sb(ctx, "h", [P, KT, L])
        x_hi = sb(ctx, "x_hi", [P, KT, L], f32r)
        x_lo = sb(ctx, "x_lo", [P, KT, L], f32r)
        raw = [sb(ctx, f"raw{s}", [P, 8, UC]) for s in range(2)]
        w_hi = [sb(ctx, f"w_hi{s}", [P, 8, UC], f32r) for s in range(2)]
        w_lo = [sb(ctx, f"w_lo{s}", [P, 8, UC], f32r) for s in range(2)]
        cst = sb(ctx, "cst", [P, NCONST])
        ident = cst[:, C_ID:C_ID + P]
        block_mean = cst[:, C_BLK:C_BLK + P]
        all_mean = cst[:, C_ONE:C_ONE + P]
        pool_fix = cst[:, C_CNT:C_CNT + 4 * PAD].rearrange("p (g t) -> p g t", g=4)
        cos, sin = cst[:, C_COS:C_COS + L], cst[:, C_SIN:C_SIN + L]
        rinv = sb(ctx, "rinv", [P, L])
        sumsq = sb(ctx, "sumsq", [P, L])
        sq = sb(ctx, "sq", [P, 2, L])
        q_sin, q_cos = sq[:, 0], sq[:, 1]
        ms_work = sb(ctx, "ms_work", [P, L])
        par_all = sb(ctx, "par_all", [P, DEPTH, NPAR])
        sink_all = sb(ctx, "sink_all", [P, DEPTH, 4])
        gains_all = sb(ctx, "gains_all", [P, DEPTH + 1, KT])
        gain_next = sb(ctx, "gain_next", [P, KT])
        par = sb(ctx, "par", [P, NPAR])
        nsink = sb(ctx, "nsink", [P, 4])
        eps = sb(ctx, "eps", [P, 1])

        with ExitStack() as sc:
            q_rot = sb(sc, "q_rot", [P, N_KV_HEADS, NB, 2 * CHUNK])
            k_dup = sb(sc, "k_dup", [P, N_KV_HEADS, L])
            v_T = sb(sc, "v_T", [P, L])
            v_win = sb(sc, "v_win", [P, NWIN, P])
            v_meta = sb(sc, "v_meta", [N_META, P])
            u_sb = sb(sc, "u_sb", [P, 2, PAD + L])
            run_a = sb(sc, "run_a", [P, PAD + L])
            run_b = sb(sc, "run_b", [P, PAD + L])
            pooled = sb(sc, "pooled", [P, 2, L])
            pool_hi = sb(sc, "pool_hi", [P, 2, L], f32r)
            pool_lo = sb(sc, "pool_lo", [P, 2, L], f32r)
            mix_hi = sb(sc, "mix_hi", [P, KT, L], f32r)
            mix_lo = sb(sc, "mix_lo", [P, KT, L], f32r)
            head = sb(sc, "head", [P, 2, L])
            head_sq = sb(sc, "head_sq", [P, NB, 2 * CHUNK])
            q_scale = sb(sc, "q_scale", [P, NB, 2, N_KV_HEADS])
            sine = v_T[:]
            rot_c = sb(sc, "rot_c", [P, L])
            rot_s = sb(sc, "rot_s", [P, L])
            k_win = sb(sc, "k_win", [P, N_KV_HEADS, NWIN, NKEY])
            probs = sb(sc, "probs", [P, 2, 4, NKEY])
            probs_win = sb(sc, "probs_win", [P, 2, 4 * P])
            probs_meta = sb(sc, "probs_meta", [N_META, 2, 4 * P])
            nmax = sb(sc, "nmax", [P, 2, 4])
            nm = sb(sc, "nm", [P, 2, 4])
            sink_arg = sb(sc, "sink_arg", [P, 2, 4])
            sink_exp = sb(sc, "sink_exp", [P, 2, 4])
            row_sum = sb(sc, "row_sum", [P, 2, 4])
            den = sb(sc, "den", [P, 2, 4])
            rden = sb(sc, "rden", [P, 2, 4])
        with ExitStack() as sc:
            m_hi = sb(sc, "m_hi", [P, FT, L], f32r)
            m_lo = sb(sc, "m_lo", [P, FT, L], f32r)
            gate = [sb(sc, f"gate{c}", [P, 2 + L]) for c in range(2)]
            conv = [sb(sc, f"conv{c}", [P, L]) for c in range(2)]
            up = [sb(sc, f"up{c}", [P, L]) for c in range(2)]
            cpar = sb(sc, "cpar", [P, 4, 2])
        with ExitStack() as sc:
            x_in = sb(sc, "x_in", [P, SEQ // P, D_MODEL])
            meta_in = sb(sc, "meta_in", [N_META, D_MODEL])
            par_in = sb(sc, "par_in", [NPAR, DEPTH, P])
            sink_in = sb(sc, "sink_in", [P, DEPTH, 2, 2])
            y_out = sb(sc, "y_out", [P, SEQ // P, D_MODEL])

        slot = [ctx.enter_context(nc.psum_tensor(f"slot{s}", [P, 2, 512], f32)) for s in range(4)]

        side = slot[3][:, 1, 0:HALF]

        def halves(s):
            return slot[s][:, :, 0:HALF]

        def tok(ap):
            return ap.rearrange("p (a t) -> p a t", a=2)

        x_loaded = [sem(f"x_loaded{t}") for t in range(SEQ // P)]
        meta_loaded, const_loaded, par_loaded = sem("meta_loaded"), sem("const_loaded"), sem("par_loaded")
        ident_loaded, sink_loaded = sem("ident_loaded"), sem("sink_loaded")
        raw_loaded = [sem("raw_loaded0"), sem("raw_loaded1")]
        hi_split = [sem("hi_split0"), sem("hi_split1")]
        lo_split = [sem("lo_split0"), sem("lo_split1")]
        down_used = sem("down_used")
        filled = [sem(f"filled{s}") for s in range(5)]
        evac = [sem(f"evac{s}") for s in range(5)]
        eps_ready = sem("eps_ready")
        par_ready = sem("par_ready")
        gains_ready = sem("gains_ready")
        xhi_ready, xlo_ready = sem("xhi_ready"), sem("xlo_ready")
        sq_ready = sem("sq_ready")
        sq_added = sem("sq_added")
        run_ready = sem("run_ready")
        pooled_ready = sem("pooled_ready")
        phi_ready, plo_ready = sem("phi_ready"), sem("plo_ready")
        headsq_ready = sem("headsq_ready")
        headn_ready = sem("headn_ready")
        qtab_ready = sem("qtab_ready")
        sine_ready = sem("sine_ready")
        rots_ready = sem("rots_ready")
        q_ready = sem("q_ready")
        rotc_ready = sem("rotc_ready")
        k_ready = sem("k_ready")
        kwin_ready = sem("kwin_ready")
        nm_ready = sem("nm_ready")
        probs_ready = sem("probs_ready")
        meta_out = sem("meta_out")
        mixhi_ready = sem("mixhi_ready")
        tap2_ready = sem("tap2_ready")
        conv_ready = sem("conv_ready")
        gelu_ready = sem("gelu_ready")
        m_ready = sem("m_ready")
        mhi_ready, mlo_ready = sem("mhi_ready"), sem("mlo_ready")
        dve_par, dve_rot, dve_attn, dve_ffn = sem("dve_par"), sem("dve_rot"), sem("dve_attn"), sem("dve_ffn")
        pool_run, pool_rot, act_log = sem("pool_run"), sem("pool_rot"), sem("act_log")
        y_ready, y_stored = [sem("y_ready0"), sem("y_ready1")], [sem("y_stored0"), sem("y_stored1")]

        MIX_ORDER = ["heads0", "heads1", "heads2", "pool3", "heads3", "heads4", "heads5", "pool2", "heads6",
                     "pool1", "heads7", "heads8", "pool0"]

        def mix_count(l, name):
            return l * len(MIX_ORDER) + (MIX_ORDER.index(name) + 1)

        ROTATED = ["q0", "k", "q1", "q2", "q3"]

        GROUPS = (3, 2, 1, 0)
        HALF_TILES = [(g, half) for g in GROUPS[1:] for half in range(2)]
        SIDE_ENDS = [5, 8, 14, 20, 26, 32, 38, 44, 48, 48, 48, 48, 48]
        POOLED_AT, POOL_HI_AT, POOL_LO_AT, MAP_AT = (1, 4, 6, 9), (2, 5, 7, 9), (3, 6, 9, 9), (5, 8, 9, 10)

        def side_rows(step):
            return (SIDE_ENDS[step] if step >= 0 else 0), SIDE_ENDS[step + 1]

        def side_name(i):
            g, half = HALF_TILES[i]
            return f"u{g}{'ab'[half]}"

        def side_done(step):
            for i in range(len(HALF_TILES)):
                if side_rows(step)[0] < (i + 1) * KT <= side_rows(step)[1]:
                    return i
            return None

        def rotated_before(l, n):
            name = ROTATED[n - 1]
            return (k_ready, l + 1) if name == "k" else (q_ready, l * 4 + (int(name[1]) + 1))

        class Chain:
            def __init__(self, eng, semaphore, turn, per):
                self.eng, self.sem, self.base, self.per, self.n = eng, semaphore, turn * per, per, 0

            def link(self, ins):
                self.n += 1
                ins.then_inc(self.sem, 1)
                self.eng.wait_ge(self.sem, self.base + self.n)

            def close(self):
                assert self.n == self.per, (self.n, self.per)

        def slot_turn(l, unit, pairs=0):
            return l * (UNITS // 2) + pairs + unit // 2

        def unit_rows(unit):
            if unit == U_POOL:
                return 2
            if unit >= U_DOWN:
                a, b = DOWN_K[(unit - U_DOWN) % 3]
                return b - a
            return 8

        def last_user_done(l, unit, i=0):
            old = unit - 2
            if old < 0:
                if old + UNITS == UNITS - 1:
                    name = f"down{KT - 1}"
                    return filled[ps.slot(name)], ps.before_last_layer(name, l) + 1
                return down_used, l * KT + 1
            if old >= U_DOWN:
                j, n = divmod(old - U_DOWN, 3)
                if n < 2:
                    return down_used, l * KT + (2 * j + n + 2)
                name = f"down{2 * j + 1}"
            elif old >= U_FFN:
                name = "gate1" if old == U_FFN else "up1"
            elif old >= U_OUT:
                name = f"out{2 * (old - U_OUT) + 1}"
            else:
                name = ("v", "q1", "q3", "u2b", "u0b", "pool0")[old]
            return filled[ps.slot(name)], ps.before(name, l, i) + 1

        def split_hi(act, l, unit, i=0, half=None):
            s, t, nk = unit % 2, slot_turn(l, unit, i), unit_rows(unit)
            a, b = (0, nk) if half is None else (half * nk // 2, (half + 1) * nk // 2)
            act.wait_ge(*last_user_done(l, unit, i))
            act.wait_ge(raw_loaded[s], t * 32 + 32)
            ins = nc.scalar.activation(w_hi[s][:, a:b], raw[s][:, a:b], ACT.Copy)
            if b == nk:
                ins.then_inc(hi_split[s], 1)

        def split_lo(dve, l, unit, i=0, half=None):
            s, t, nk = unit % 2, slot_turn(l, unit, i), unit_rows(unit)
            a, b = (0, nk) if half is None else (half * nk // 2, (half + 1) * nk // 2)
            dve.wait_ge(hi_split[s], t + 1)
            ins = nc.vector.tensor_tensor(w_lo[s][:, a:b], raw[s][:, a:b], w_hi[s][:, a:b].bitcast(f32), ALU.subtract)
            if b == nk:
                ins.then_inc(lo_split[s], 1)

        def h_from_layer_before(l, k):
            name = f"down{k}"
            return evac[ps.slot(name)], ps.before_last_layer(name, l) + 1

        def blocks(weights):
            return weights.rearrange("(k p) c -> p k c", p=P)

        BLOCKS = [(0, N_META), (N_META, N_META + CHUNK)] + [(N_META + c * CHUNK, NKEY) for c in range(1, NCH)]

        block = ctx.enter_context(nc.Block())

        @block.sync
        def _(sp):
            sp.dma_start(cst[:, 0:C_CNT], const[:, 0:C_CNT]).then_inc(ident_loaded, 16)
            for t in range(SEQ // P):
                sp.dma_start(x_in[:, t], x[0, t * P:(t + 1) * P, :]).then_inc(x_loaded[t], 16)

            def load(l, unit, src, i=0):
                s, n = unit % 2, unit_rows(unit)
                parts = [(raw[s][:, a:a + n // 2], src[:, a:a + n // 2]) for a in (n // 2, 0)]
                sp.wait_ge(lo_split[s], slot_turn(l, unit, i) + 1)
                for dst, part in parts:
                    sp.dma_start(dst, part).then_inc(raw_loaded[s], 16)

            sp.wait_ge(par_loaded, 16 * 11)
            with sp.Fori(0, DEPTH) as l:
                win, wo, wd = blocks(w_in[l]), blocks(w_out[l]), blocks(w_down[l])
                wg, wu = blocks(w_gate[l]), blocks(w_up[l])
                load(l, U_KV, win[:, :, ATTN_WIDTH:ATTN_WIDTH + UC])
                for j in range(2):
                    load(l, U_Q + j, win[:, :, j * UC:(j + 1) * UC])
                col_u = ATTN_WIDTH + 2 * KV_WIDTH
                load(l, U_U23, win[:, :, col_u + UC:col_u + 2 * UC])
                load(l, U_U01, win[:, :, col_u:col_u + UC])
                s = U_POOL % 2
                sp.wait_ge(lo_split[s], slot_turn(l, U_POOL) + 1)
                flat = w_pool.rearrange("l g c d -> (l g c) d")
                for g in range(2):
                    rows = flat[bass.ds(l * (4 * P) + g * (2 * P), 2 * P)]
                    sp.dma_start(raw[s][:, g].rearrange("p (g d) -> p g d", g=2),
                                 rows.rearrange("(g c) d -> c g d", g=2)).then_inc(raw_loaded[s], 16)
                for j in range(D_MODEL // UC):
                    load(l, U_OUT + j, wo[:, :, j * UC:(j + 1) * UC])
                with sp.Fori(0, FI) as i:
                    load(l, U_FFN, wg[:, :, bass.ds(i * UC, UC)], i)
                    load(l, U_FFN + 1, wu[:, :, bass.ds(i * UC, UC)], i)
                for j in range(D_MODEL // UC):
                    for n, (a, b) in enumerate(DOWN_K):
                        load(l, U_DOWN + 3 * j + n, wd[:, a:b, j * UC:(j + 1) * UC])
            for t in range(SEQ // P):
                for half in range(2):
                    sp.wait_ge(y_ready[half], t + 1)
                    cols = slice(half * 512, (half + 1) * 512)
                    sp.dma_start(out[0, t * P:(t + 1) * P, cols], y_out[:, t, cols]).then_inc(y_stored[half], 16)
            for half in range(2):
                sp.wait_ge(y_stored[half], 16 * (SEQ // P))

        @block.tensor
        def _(pe):
            def open_slot(name, l, turn=0):
                s = ps.slot(name)
                pe.wait_ge(evac[s], ps.before(name, l, turn))
                return s

            def dense(s, ws, col, rows, a_hi, a_lo, first=True, last=True, ready=None, part=None):
                dst = [(half, slot[s][:, half, 0:HALF]) for half in range(2)] if part is None else [(part, side)]
                for n, (r, k) in enumerate(rows):
                    if ready is not None:
                        ready(k)
                    end = last and n == len(rows) - 1
                    cols = slice(col, col + P)
                    for w, a in ((w_hi, a_hi), (w_hi, a_lo), (w_lo, a_hi)):
                        for half, out_half in dst:
                            ins = nc.tensor.matmul(out_half, w[ws][:, r, cols],
                                                   a[:, k, half * HALF:(half + 1) * HALF],
                                                   start=first and n == 0 and w is w_hi and a is a_hi,
                                                   stop=end and w is w_lo)
                return ins

            def column_mean(name, l, weights, src, semaphore, count):
                s = open_slot(name, l)
                pe.wait_ge(semaphore, count)
                for half in range(2):
                    ins = nc.tensor.matmul(slot[s][:, half, 0:HALF], weights, src[:, half * HALF:(half + 1) * HALF],
                                           start=True, stop=True)
                ins.then_inc(filled[s], 1)

            pe.sem_inc(down_used, 1)
            pe.sem_inc(filled[4], 1)
            pe.wait_ge(ident_loaded, 16)
            pe.wait_ge(meta_loaded, 16)
            for k in range(KT):
                s, feat = (2 + k) % 4, slice(k * P, (k + 1) * P)
                if k == 3:
                    pe.wait_ge(par_loaded, 16 * 11)
                    for l in range(DEPTH):
                        ins = nc.tensor.transpose(slot[s][:, l, 0:NPAR], par_in[:, l, :], ident[0:NPAR, 0:NPAR])
                    ins.then_inc(filled[s], 1)
                    pe.wait_ge(evac[s], 1)
                if k >= 4:
                    pe.wait_ge(evac[s], ps.PROLOGUE[s] - 1)
                nc.tensor.transpose(slot[s][:, 0, 0:N_META], meta_in[:, feat], ident[0:N_META, 0:N_META])
                for t in range(SEQ // P):
                    if k == 0:
                        pe.wait_ge(x_loaded[t], 16)
                    dst = slot[s][:, 0, N_META + t * P:N_META + (t + 1) * P] if t < 3 else slot[s][:, 1, 0:P]
                    ins = nc.tensor.transpose(dst, x_in[:, t, feat], ident)
                ins.then_inc(filled[s], 1)

            eight = [(k, k) for k in range(KT)]
            with pe.Fori(0, DEPTH) as l:
                def project(name, unit, ready=None):
                    c = int(name in ("v", "u3", "q1", "q3"))
                    s = open_slot(name, l)
                    if c == 0 or name == "u3":
                        pe.wait_ge(lo_split[unit % 2], slot_turn(l, unit) + 2)
                    dense(s, unit % 2, c * P, eight, x_hi, x_lo, ready=ready).then_inc(filled[s], 1)

                def q_means(kv):
                    s = open_slot(f"qn{kv}", l)
                    pe.wait_ge(headsq_ready, l * 5 + (2 * kv + 3))
                    for b in range(NB):
                        ins = nc.tensor.matmul(slot[s][:, 0, 2 * b:2 * b + 2], head_sq[:, b, :],
                                               cst[:, C_BLK:C_BLK + P:HEAD_DIM], start=True, stop=True)
                    ins.then_inc(filled[s], 1)

                project("k", U_KV, ready=lambda k: pe.wait_ge(xlo_ready, l * (2 * KT) + (k + 1)))
                project("v", U_KV)
                column_mean("attn_norm", l, all_mean, sumsq, sq_added, l * (2 * (KT - 1)) + (KT - 1))
                project("q0", U_Q)
                s = open_slot("v_T", l)
                pe.wait_ge(evac[ps.slot("v")], ps.before("v", l) + 1)
                flat = slot[s][:].rearrange("p a t -> p (a t)")
                for w in range(NWIN):
                    t0 = N_META + w * CHUNK
                    nc.tensor.transpose(flat[:, w * P:(w + 1) * P], v_T[:, t0:t0 + P], ident)
                nc.tensor.transpose(flat[0:N_META, NWIN * P:(NWIN + 1) * P], v_T[:, 0:N_META], ident)\
                  .then_inc(filled[s], 1)
                k_squares = head_sq[:].rearrange("p b q -> p (b q)")[:, 0:L]
                column_mean("k_sq", l, block_mean, k_squares, headsq_ready, l * 5 + 1)
                project("q1", U_Q)
                project("q2", U_Q + 1)
                q_means(0)
                project("q3", U_Q + 1)
                project("u3", U_U23)

                def project_side(first, last):
                    for n in range(first, last):
                        i, k = divmod(n, KT)
                        (g, half), name = HALF_TILES[i], side_name(i)
                        unit = U_U01 if g < 2 else U_U23
                        if k == 0:
                            open_slot(name, l)
                            if g == 1 and half == 0:
                                pe.wait_ge(lo_split[unit % 2], slot_turn(l, unit) + 2)
                        ins = dense(None, unit % 2, (g % 2) * P, [(k, k)], x_hi, x_lo, part=half,
                                    first=k == 0, last=k == KT - 1)
                        if k == KT - 1:
                            ins.then_inc(filled[4], 1)

                def pool_map(n):
                    g = GROUPS[n]
                    s = open_slot(f"pool{g}", l)
                    if n == 0:
                        pe.wait_ge(lo_split[U_POOL % 2], slot_turn(l, U_POOL) + 2)
                    pe.wait_ge(plo_ready, l * 4 + (n + 1))
                    dense(s, U_POOL % 2, (g % 2) * P, [(g // 2, n % 2)], pool_hi, pool_lo).then_inc(filled[s], 1)

                def scores(b):
                    q0, nk = BLOCKS[b]
                    s = open_slot(f"scores{b}", l)
                    if b == 0:
                        pe.wait_ge(k_ready, l + 1)
                        pe.wait_ge(q_ready, l * 4 + 4)
                    if b == 2:
                        pe.wait_ge(kwin_ready, l + 1)
                    for t in range(4):
                        j2, kv = divmod(t, 2)
                        part = slice(j2 * HEAD_DIM, (j2 + 1) * HEAD_DIM)
                        keys = k_dup[part, kv, 0:nk] if b < 2 else k_win[part, kv, b - 2, :]
                        ins = nc.tensor.matmul(slot[s][:, j2, kv * nk:(kv + 1) * nk], q_rot[part, kv, b], keys,
                                               start=True, stop=True)
                    ins.then_inc(filled[s], 1)

                def probs_T(b):
                    nk = BLOCKS[b][1]
                    s = open_slot(f"probs_T{b}", l)
                    if b > 1:
                        pe.wait_ge(meta_out, l * (NB - 1) + (b - 1))
                    pe.wait_ge(probs_ready, l * NB + (b + 1))
                    for t in range(4):
                        ins = nc.tensor.transpose(slot[s][0:N_META, 1, t * P:(t + 1) * P],
                                                  probs[:, b % 2, t, 0:N_META], ident)
                        if nk > N_META:
                            ins = nc.tensor.transpose(slot[s][0:nk - N_META, 0, t * P:(t + 1) * P],
                                                      probs[:, b % 2, t, N_META:nk], ident)
                    ins.then_inc(filled[s], 1)

                def heads(b):
                    n = BLOCKS[b][1] - N_META
                    s = open_slot(f"heads{b}", l)
                    name = f"probs_T{b}"
                    pe.wait_ge(evac[ps.slot(name)], ps.before(name, l) + 1)
                    if b > 0:
                        pe.wait_ge(meta_out, l * (NB - 1) + b)
                    for t in range(4):
                        j2, kv = divmod(t, 2)
                        dst = slot[s][j2 * HEAD_DIM:(j2 + 1) * HEAD_DIM, 0, kv * P:(kv + 1) * P]
                        dims, cols = slice(kv * HEAD_DIM, (kv + 1) * HEAD_DIM), slice(t * P, (t + 1) * P)
                        ins = nc.tensor.matmul(dst, v_meta[:, dims], probs_meta[:, b % 2, cols],
                                               start=True, stop=n == 0)
                        if n > 0:
                            ins = nc.tensor.matmul(dst, v_win[0:n, max(b - 2, 0), dims], probs_win[0:n, b % 2, cols],
                                                   start=False, stop=True)
                    ins.then_inc(filled[s], 1)

                name = "heads0"
                pe.wait_ge(evac[ps.slot(name)], ps.before(name, l))
                project_side(*side_rows(-1))
                q_means(1)
                for step in range(NB + 2):
                    if step < NB:
                        scores(step)
                    for n in (0, 1):
                        if step == MAP_AT[n]:
                            pool_map(n)
                    first, end = side_rows(step)
                    done = side_done(step)
                    cut = (first + end) // 2 if done is None else (done + 1) * KT
                    project_side(first, min(cut, end))
                    if step >= 2:
                        heads(step - 2)
                    if step == MAP_AT[2]:
                        pool_map(2)
                    if 1 <= step <= NB:
                        probs_T(step - 1)
                    project_side(cut, end)
                    if step == MAP_AT[3]:
                        pool_map(3)

                rows = [(k, k) for k in (7, 6, 5, 0, 1, 2, 3, 4)]

                def mixed(k):
                    if k == 7:
                        pe.wait_ge(meta_out, l * (NB - 1) + (NB - 1))
                    if k >= 4:
                        name = f"pool{k - 4}"
                        pe.wait_ge(evac[ps.slot(name)], ps.before(name, l) + 1)
                    if k == 0:
                        name = f"heads{NB - 1}"
                        pe.wait_ge(evac[ps.slot(name)], ps.before(name, l) + 1)

                with pe.Fori(0, 2) as i:
                    for t in range(4):
                        s, unit = open_slot(f"out{t}", l, i), U_OUT + t // 2
                        if t % 2 == 0:
                            pe.wait_ge(lo_split[unit % 2], slot_turn(l, unit, i) + 2)
                        dense(s, unit % 2, (t % 2) * P, rows, mix_hi, mix_lo, ready=mixed if t == 0 else None)\
                          .then_inc(filled[s], 1)

                def mlp_tiles(i, ready=None):
                    for n, name in enumerate(("gate0", "gate1", "up0", "up1")):
                        s, unit = open_slot(name, l, i), U_FFN + n // 2
                        if n % 2 == 0:
                            pe.wait_ge(lo_split[unit % 2], slot_turn(l, unit, i) + 2)
                        dense(s, unit % 2, (n % 2) * P, eight, x_hi, x_lo,
                              ready=ready if n == 0 else None).then_inc(filled[s], 1)
                        if n == 0 and ready is not None:
                            column_mean("ffn_norm", l, all_mean, sumsq, sq_added,
                                        l * (2 * (KT - 1)) + 2 * (KT - 1))

                mlp_tiles(0, ready=lambda k: pe.wait_ge(xlo_ready, l * (2 * KT) + (KT + k + 1)))
                with pe.Fori(1, FI) as i:
                    mlp_tiles(i)
                with pe.Fori(0, 2) as i:
                    for j in range(2):
                        for n, (a, b) in enumerate(DOWN_K):
                            unit = U_DOWN + 3 * j + n
                            for c in range(2):
                                name = f"down{2 * j + c}"
                                s = open_slot(name, l, i) if n == 0 else ps.slot(name)
                                if c == 0:
                                    pe.wait_ge(lo_split[unit % 2], slot_turn(l, unit, i * 3) + 2)
                                    pe.wait_ge(mlo_ready, l * FT + b)
                                ins = dense(s, unit % 2, c * P, [(k - a, k) for k in range(a, b)],
                                            m_hi, m_lo, first=n == 0, last=n == 2)
                                if n == 2:
                                    ins.then_inc(filled[s], 1)
                                elif c == 1:
                                    ins.then_inc(down_used, 1)

            for s in range(4):
                pe.wait_ge(evac[s], ps.PROLOGUE[s] + ps.uses[s] * DEPTH)
            for t in range(SEQ // P):
                t0 = N_META + t * P
                for k in range(KT):
                    ins = nc.tensor.transpose(slot[t][:, k // 4, (k % 4) * P:(k % 4 + 1) * P], h[:, k, t0:t0 + P], ident)
                ins.then_inc(filled[t], 1)

        @block.gpsimd
        def _(pool):
            def sum_squares(norm):
                for k in range(1, KT):
                    pool.wait_ge(sq_ready, norm * KT + (k + 1))
                    if k == 1:
                        ins = nc.gpsimd.tensor_tensor(sumsq[:], sq[:, 0], sq[:, 1], ALU.add)
                    else:
                        pool.wait_ge(sq_added, norm * (KT - 1) + (k - 1))
                        ins = nc.gpsimd.tensor_tensor(sumsq[:], sumsq[:], sq[:, k % 2], ALU.add)
                    ins.then_inc(sq_added, 1)

            pool.wait_ge(const_loaded, 16)
            with pool.Fori(0, DEPTH) as l:
                pool.wait_ge(hi_split[0], slot_turn(l, 0) + 1)
                nc.gpsimd.tensor_tensor(w_lo[0][:], raw[0][:], w_hi[0][:].bitcast(f32), ALU.subtract)\
                  .then_inc(lo_split[0], 1)
                sum_squares(l * 2)
                pads = Chain(pool, pool_run, l, 1)
                nc.gpsimd.memset(u_sb[:, :, 0:PAD], 0.0)
                nc.gpsimd.memset(run_a[:, 0:PAD], 0.0)
                pads.link(nc.gpsimd.memset(run_b[:, 0:PAD], 0.0))
                steps = Chain(pool, pool_rot, l, 10 + 4)

                def rotated(n):
                    name = ROTATED[n]
                    if n > 0:
                        pool.wait_ge(*rotated_before(l, n))
                    if name == "k":
                        pool.wait_ge(headn_ready, l + 1)
                        nc.gpsimd.tensor_tensor(rot_c[:], k_dup[:, 0], cos, ALU.mult).then_inc(rotc_ready, 1)
                        return
                    j = int(name[1])
                    pool.wait_ge(evac[ps.slot(name)], ps.before(name, l) + 1)
                    pool.wait_ge(qtab_ready, l + 1)
                    steps.link(nc.gpsimd.tensor_tensor(rot_c[:], head[:, j % 2], q_cos, ALU.mult))
                    pool.wait_ge(rots_ready, l * 5 + (n + 1))
                    kv, cols = j // 2, slice(j % 2 * CHUNK, (j % 2 + 1) * CHUNK)
                    chunks = [r[:, N_META:].rearrange("p (b q) -> p b q", q=CHUNK) for r in (rot_c, rot_s)]
                    nc.gpsimd.tensor_tensor(q_rot[:, kv, 0, cols], rot_c[:, 0:CHUNK], rot_s[:, 0:CHUNK], ALU.add)
                    nc.gpsimd.tensor_tensor(q_rot[:, kv, 1:, cols], *chunks, ALU.add).then_inc(q_ready, 1)

                def group(n):
                    g = GROUPS[n]
                    name = f"u{g}b" if n else "u3"
                    pool.wait_ge(evac[ps.slot(name)], ps.before(name, l) + 1)
                    if n > 0:
                        pool.wait_ge(pooled_ready, l * 4 + n)
                    src, step = u_sb[:, n % 2], 1
                    for m in range(g + 1):
                        dst = (run_a, run_b)[(m + g) % 2]
                        steps.link(nc.gpsimd.tensor_tensor(dst[:, PAD:], src[:, PAD:],
                                                           src[:, PAD - step:PAD + L - step], ALU.add))
                        src, step = dst[:, :], step * 2
                    nc.gpsimd.tensor_tensor(run_a[:, PAD:2 * PAD], run_a[:, PAD:2 * PAD], pool_fix[:, g],
                                            ALU.mult).then_inc(run_ready, 1)

                for n in range(5):
                    rotated(n)
                for n in range(4):
                    group(n)
                steps.close()
                sum_squares(l * 2 + 1)
                with pool.Fori(0, FI) as i:
                    for c in range(2):
                        u = ps.slot(f"up{c}")
                        pool.wait_ge(gelu_ready, l * FT + i * 2 + (c + 1))
                        pool.wait_ge(evac[u], ps.before(f"up{c}", l, i) + 1)
                        nc.gpsimd.tensor_tensor(up[c][:], up[c][:], conv[c][:], ALU.mult).then_inc(m_ready, 1)

        @block.scalar
        def _(act):
            act.dma_start(meta_in[:], meta_tokens).then_inc(meta_loaded, 16)
            by_row = "l (r p) -> r l p"
            for src, r, n in ((attn_norm_g, R_AG, KT), (ffn_norm_g, R_FG, KT), (pool_scale, R_PS, 4),
                              (conv_b, R_CB, FT), (conv_w[:, 0], R_CW, FT), (conv_w[:, 1], R_CW + FT, FT),
                              (conv_w[:, 2], R_CW + 2 * FT, FT)):
                act.dma_start(par_in[r:r + n], src.rearrange(by_row, p=P)).then_inc(par_loaded, 16)
            for src, r in ((q_norm_g, R_QG), (k_norm_g, R_KG)):
                for half in range(2):
                    act.dma_start(par_in[r:r + 1, :, half * HEAD_DIM:(half + 1) * HEAD_DIM],
                                  src.rearrange("(a l) d -> a l d", a=1)).then_inc(par_loaded, 16)
            for l in range(DEPTH):
                for jp in range(2):
                    act.dma_start(sink_in[jp * 64:(jp + 1) * 64, l],
                                  sinks[l].rearrange("(kv jp j) -> jp kv j", jp=2, j=2)[jp]
                                  .partition_broadcast(64)).then_inc(sink_loaded, 16)
            act.dma_start(cst[:, C_CNT:], const[:, C_CNT:]).then_inc(const_loaded, 16)

            def gain_hi(k, ready, gains):
                act.wait_ge(*ready)
                nc.scalar.activation(x_hi[:, k], h[:, k], ACT.Copy, scale=gains[:, k:k + 1])\
                  .then_inc(xhi_ready, 1)

            act.wait_ge(eps_ready, 1)
            with act.Fori(0, DEPTH) as l:
                roots = Chain(act, act_log, l, 2)

                def square(norm, k):
                    if k >= 2:
                        act.wait_ge(sq_added, (l * 2 + norm) * (KT - 1) + max(1, k - 2))
                    nc.scalar.activation(sq[:, k % 2], h[:, k], ACT.Square).then_inc(sq_ready, 1)

                def root(name, dst):
                    s = ps.slot(name)
                    act.wait_ge(filled[s], ps.before(name, l) + 1)
                    roots.link(nc.scalar.activation(tok(ms_work[:]), halves(s), ACT.Ln, bias=eps[:]))
                    nc.scalar.activation(dst, ms_work[:], ACT.Exp, scale=-0.5).then_inc(evac[s], 1)

                def q_squares(j):
                    name = f"q{j}"
                    act.wait_ge(evac[ps.slot(name)], ps.before(name, l) + 1)
                    if j == 2:
                        act.wait_ge(filled[ps.slot("qn0")], ps.before("qn0", l) + 1)
                    cols = slice(j % 2 * CHUNK, (j % 2 + 1) * CHUNK)
                    nc.scalar.activation(head_sq[:, 0, cols], head[:, j % 2, 0:CHUNK], ACT.Square)
                    nc.scalar.activation(head_sq[:, 1:, cols],
                                         head[:, j % 2, N_META:].rearrange("p (b q) -> p b q", q=CHUNK), ACT.Square)\
                      .then_inc(headsq_ready, 1)

                def q_rms(kv):
                    s = ps.slot(f"qn{kv}")
                    act.wait_ge(filled[s], ps.before(f"qn{kv}", l) + 1)
                    nc.scalar.activation(q_scale[:, :, :, kv], slot[s][:, 0, 0:2 * NB].rearrange("p (b j) -> p b j", j=2),
                                         ACT.Sqrt, bias=eps[:]).then_inc(evac[s], 1)

                def shift(n):
                    act.wait_ge(sine_ready, l * 5 + (n + 1))
                    if n > 0:
                        act.wait_ge(*rotated_before(l, n))
                    for to, fr in ((0, 32), (32, 0), (64, 96), (96, 64)):
                        ins = nc.scalar.activation(rot_s[to:to + 32], sine[fr:fr + 32], ACT.Copy)
                    ins.then_inc(rots_ready, 1)

                def pooled_hi(n):
                    act.wait_ge(pooled_ready, l * 4 + (n + 1))
                    if n >= 2:
                        name = f"pool{GROUPS[n - 2]}"
                        act.wait_ge(filled[ps.slot(name)], ps.before(name, l) + 1)
                    nc.scalar.activation(pool_hi[:, n % 2], pooled[:, n % 2], ACT.Copy).then_inc(phi_ready, 1)

                def pool_map_hi(n):
                    g = GROUPS[n]
                    s = ps.slot(f"pool{g}")
                    act.wait_ge(filled[s], ps.before(f"pool{g}", l) + 1)
                    nc.scalar.activation(tok(mix_hi[:, 4 + g]), halves(s), ACT.Copy,
                                         scale=par[:, R_PS + g:R_PS + g + 1]).then_inc(mixhi_ready, 1)

                split_hi(act, l, 0)
                act.wait_ge(gains_ready, l + 1)
                for k in range(KT):
                    gain_hi(k, h_from_layer_before(l, k), gain_next)
                for k in range(KT):
                    square(0, k)
                split_hi(act, l, 1)
                split_hi(act, l, 2)
                root("attn_norm", rinv[:])
                act.wait_ge(evac[ps.slot("k")], ps.before("k", l) + 1)
                nc.scalar.activation(head_sq[:].rearrange("p b q -> p (b q)")[:, 0:L], k_dup[:, 0], ACT.Square)\
                  .then_inc(headsq_ready, 1)
                act.wait_ge(par_ready, l * 2 + 2)
                nc.scalar.activation(q_sin, sin, ACT.Copy, scale=par[:, R_QG:R_QG + 1])
                nc.scalar.activation(q_cos, cos, ACT.Copy, scale=par[:, R_QG:R_QG + 1]).then_inc(qtab_ready, 1)
                s = ps.slot("v_T")
                act.wait_ge(filled[s], ps.before("v_T", l) + 1)
                flat = slot[s][:].rearrange("p a t -> p (a t)")
                nc.scalar.activation(v_meta[:], flat[0:N_META, NWIN * P:(NWIN + 1) * P], ACT.Copy)
                nc.scalar.activation(v_win[:, 0:4].rearrange("p w d -> p (w d)"), flat[:, 0:4 * P], ACT.Copy)
                nc.scalar.activation(v_win[:, 4:NWIN].rearrange("p w d -> p (w d)"), flat[:, 4 * P:NWIN * P],
                                     ACT.Copy).then_inc(evac[s], 1)
                s = ps.slot("k_sq")
                act.wait_ge(filled[s], ps.before("k_sq", l) + 1)
                nc.scalar.activation(tok(ms_work[:]), halves(s), ACT.Sqrt, bias=eps[:]).then_inc(evac[s], 1)
                q_squares(0)
                shift(0)
                shift(1)
                q_squares(1)
                split_hi(act, l, 3)
                shift(2)
                act.wait_ge(k_ready, l + 1)
                for kv in range(N_KV_HEADS):
                    nc.scalar.activation(k_win[:, kv, :, 0:N_META],
                                         k_dup[:, kv, 0:N_META].unsqueeze(1).broadcast_to([P, NWIN, N_META]), ACT.Copy)
                    keys = k_dup[:, kv, N_META:]
                    windows = bass.AP(keys.tensor, keys.offset, [list(keys.ap[0]), [CHUNK, NWIN], [1, 2 * CHUNK]])
                    ins = nc.scalar.activation(k_win[:, kv, :, N_META:], windows, ACT.Copy)
                ins.then_inc(kwin_ready, 1)
                shift(3)
                split_hi(act, l, 4)
                q_squares(2)
                q_rms(0)
                q_squares(3)
                shift(4)
                q_rms(1)

                def exps(b):
                    nk, s, y = BLOCKS[b][1], ps.slot(f"scores{b}"), b % 2
                    act.wait_ge(nm_ready, l * NB + b + 1)
                    if b >= 2:
                        old = f"probs_T{b - 2}"
                        act.wait_ge(filled[ps.slot(old)], ps.before(old, l) + 1)
                    nc.scalar.activation(sink_exp[:, y], sink_arg[:, y], ACT.Exp)
                    for t in range(4):
                        col = slice((t % 2) * nk, (t % 2 + 1) * nk)
                        ins = nc.scalar.activation(probs[:, y, t, 0:nk], slot[s][:, t // 2, col], ACT.Exp,
                                                   bias=nm[:, y, t:t + 1],
                                                   scale=q_scale[:, b, t // 2, t % 2:t % 2 + 1], accum_out=row_sum[:, y, t:t + 1])
                    ins.then_inc(evac[s], 1)

                def probs_out(b):
                    n = BLOCKS[b][1] - N_META
                    pt = ps.slot(f"probs_T{b}")
                    act.wait_ge(filled[pt], ps.before(f"probs_T{b}", l) + 1)
                    if n > 0:
                        ins = nc.scalar.activation(probs_win[0:n, b % 2], slot[pt][0:n, 0, :], ACT.Copy)
                    else:
                        ins = nc.scalar.activation(probs_meta[:, 0], slot[pt][0:N_META, 1, :], ACT.Copy)
                    ins.then_inc(evac[pt], 1)

                def heads_hi(b):
                    t0, nq = BLOCKS[b][0], CHUNK if b else N_META
                    hd = ps.slot(f"heads{b}")
                    act.wait_ge(filled[hd], ps.before(f"heads{b}", l) + 1)
                    src = slot[hd][:, 0, 0:4 * CHUNK].rearrange("p (t q) -> p t q", t=4)[:, :, 0:nq]
                    nc.scalar.activation(mix_hi[:, 0:4, t0:t0 + nq], src, ACT.Copy).then_inc(mixhi_ready, 1)

                for step in range(NB + 3):
                    if step >= 3 and step != NB:
                        heads_hi(step - 3)
                    if 2 <= step < NB + 2 and step != NB:
                        probs_out(step - 2)
                    if step == 8:
                        split_hi(act, l, U_OUT, half=0)
                    if step == NB:
                        split_hi(act, l, U_OUT, half=1)
                        pooled_hi(3)
                    for n in (0, 1, 2):
                        if step == MAP_AT[n]:
                            pool_map_hi(n)
                    if step == NB - 1:
                        heads_hi(NB - 3)
                        probs_out(NB - 2)
                    if step < NB:
                        exps(step)
                    if step in POOL_HI_AT[0:3]:
                        pooled_hi(POOL_HI_AT.index(step))
                    if step == 3:
                        split_hi(act, l, U_POOL)
                pool_map_hi(3)
                split_hi(act, l, U_OUT + 1)

                for j in range(4):
                    if j < 3:
                        split_hi(act, l, U_OUT + 2 + j)
                    for k in (2 * j, 2 * j + 1):
                        gain_hi(k, (evac[ps.slot(f"out{k}")], ps.before(f"out{k}", l) + 1),
                                par[:, R_FG:R_FG + KT])
                        square(1, k)
                split_hi(act, l, U_OUT + 5)
                root("ffn_norm", rinv[:])
                roots.close()

                with act.Fori(0, FI) as i:
                    for c in range(2):
                        g = ps.slot(f"gate{c}")
                        act.wait_ge(evac[g], ps.before(f"gate{c}", l, i) + 1)
                        nc.scalar.activation(conv[c][:], gate[c][:, 2:], ACT.Identity, bias=cpar[:, 3, c:c + 1],
                                             scale=cpar[:, 2, c:c + 1]).then_inc(tap2_ready, 1)
                    split_hi(act, l, U_FFN + 2, i)
                    for c in range(2):
                        act.wait_ge(conv_ready, l * FT + i * 2 + (c + 1))
                        nc.scalar.activation(conv[c][:], conv[c][:], ACT.Gelu).then_inc(gelu_ready, 1)
                    split_hi(act, l, U_FFN + 3, i)
                    for c in range(2):
                        act.wait_ge(m_ready, l * FT + i * 2 + (c + 1))
                        nc.scalar.activation(m_hi[:, bass.ds(i * 2 + c, 1)].rearrange("p a t -> p (a t)"),
                                             up[c][:], ACT.Copy).then_inc(mhi_ready, 1)
                for unit in range(U_DOWN + 2, UNITS):
                    split_hi(act, l, unit)

            for t in range(SEQ // P):
                act.wait_ge(filled[t], ps.PROLOGUE[t] + ps.uses[t] * DEPTH + 1)
                nc.scalar.activation(y_out[:, t, 0:512], slot[t][:, 0, :], ACT.Copy).then_inc(y_ready[0], 1)

        @block.vector
        def _(dve):
            for s in range(2):
                dve.sem_inc(lo_split[s], 1)
            dve.sem_inc(evac[4], 1)
            nc.vector.memset(eps[:], EPS).then_inc(eps_ready, 1)
            prep = Chain(dve, dve_par, 0, 4)
            for k in range(KT):
                s, cut = (2 + k) % 4, N_META + 3 * P
                if k == 3:
                    dve.wait_ge(filled[s], 1)
                    nc.vector.tensor_copy(par_all[:], slot[s][:, :, 0:NPAR]).then_inc(evac[s], 1)
                    dve.wait_ge(evac[s], 1)
                    prep.link(nc.vector.memset(gains_all[:, DEPTH], 0.0))
                    prep.link(nc.vector.tensor_copy(gains_all[:, 0:DEPTH], par_all[:, :, R_AG:R_AG + KT]))
                    nc.vector.tensor_copy(gain_next[:], par_all[:, 0, R_AG:R_AG + KT]).then_inc(gains_ready, 1)
                dve.wait_ge(filled[s], ps.PROLOGUE[s] - (k < 4))
                nc.vector.tensor_copy(h[:, k, 0:cut], slot[s][:, 0, 0:cut])
                nc.vector.tensor_copy(h[:, k, cut:L], slot[s][:, 1, 0:P]).then_inc(evac[s], 1)
            dve.wait_ge(sink_loaded, 16 * 2 * DEPTH)
            prep.link(nc.vector.tensor_scalar(sink_all[:].rearrange("p l (j kv) -> p l j kv", j=2),
                                              sink_in[:].rearrange("p l kv j -> p l j kv"), -1.0, None, ALU.mult))
            prep.link(nc.vector.tensor_scalar(par_all[:, :, R_QG:R_QG + 1], par_all[:, :, R_QG:R_QG + 1],
                                              float(HEAD_DIM) ** -0.5, None, ALU.mult))
            prep.close()
            dve.wait_ge(const_loaded, 16)

            def gain_lo(k, count, gains):
                dve.wait_ge(xhi_ready, count)
                nc.vector.scalar_tensor_tensor(x_lo[:, k], h[:, k], gains[:, k:k + 1],
                                               x_hi[:, k].bitcast(f32), ALU.mult, ALU.subtract)\
                  .then_inc(xlo_ready, 1)

            with dve.Fori(0, DEPTH) as l:
                dve.wait_ge(gains_ready, l + 1)
                for k in range(KT):
                    gain_lo(k, l * (2 * KT) + (k + 1), gain_next)
                nc.vector.tensor_copy(par[:], par_all[:, bass.ds(l, 1)].rearrange("p a r -> p (a r)"))\
                  .then_inc(par_ready, 1)
                nc.vector.tensor_copy(nsink[:], sink_all[:, bass.ds(l, 1)].rearrange("p a r -> p (a r)"))\
                  .then_inc(par_ready, 1)
                split_lo(dve, l, 1)
                split_lo(dve, l, 2)

                def inverse_rms_ready(name):
                    dve.wait_ge(evac[ps.slot(name)], ps.before(name, l) + 1)

                def scaled(name, dst, turn=0):
                    s = ps.slot(name)
                    dve.wait_ge(filled[s], ps.before(name, l, turn) + 1)
                    nc.vector.tensor_tensor(tok(dst), halves(s), tok(rinv[:]), ALU.mult).then_inc(evac[s], 1)

                def q_tile(j):
                    if j >= 2:
                        dve.wait_ge(q_ready, l * 4 + (j - 1))
                    scaled(f"q{j}", head[:, j % 2])

                rot = Chain(dve, dve_rot, l, 2)

                def sine_part(n):
                    name = ROTATED[n]
                    if n > 0:
                        dve.wait_ge(rots_ready, l * 5 + n)
                    if name == "k":
                        dve.wait_ge(headn_ready, l + 1)
                        nc.vector.tensor_tensor(sine, k_dup[:, 0], sin, ALU.mult).then_inc(sine_ready, 1)
                        return
                    dve.wait_ge(evac[ps.slot(name)], ps.before(name, l) + 1)
                    nc.vector.tensor_tensor(sine, head[:, int(name[1]) % 2], q_sin, ALU.mult).then_inc(sine_ready, 1)

                def pooled_tile(n):
                    dve.wait_ge(run_ready, l * 4 + (n + 1))
                    if n >= 2:
                        dve.wait_ge(plo_ready, l * 4 + (n - 1))
                    nc.vector.scalar_tensor_tensor(pooled[:, n % 2], run_a[:, PAD:], 1.0 / POOL_SIZES[GROUPS[n]],
                                                   u_sb[:, n % 2, PAD:], ALU.mult, ALU.subtract)\
                      .then_inc(pooled_ready, 1)

                def pooled_lo(n):
                    dve.wait_ge(phi_ready, l * 4 + (n + 1))
                    nc.vector.tensor_tensor(pool_lo[:, n % 2], pooled[:, n % 2], pool_hi[:, n % 2].bitcast(f32),
                                            ALU.subtract).then_inc(plo_ready, 1)

                dve.wait_ge(par_ready, l * 2 + 2)
                inverse_rms_ready("attn_norm")
                scaled("k", k_dup[:, 0])
                scaled("v", v_T[:])
                q_tile(0)
                dve.wait_ge(qtab_ready, l + 1)
                dve.wait_ge(evac[ps.slot("v_T")], ps.before("v_T", l) + 1)
                sine_part(0)
                dve.wait_ge(evac[ps.slot("k_sq")], ps.before("k_sq", l) + 1)
                rot.link(nc.vector.reciprocal(ms_work[:], ms_work[:]))
                nc.vector.scalar_tensor_tensor(k_dup[:, 0], k_dup[:, 0], par[:, R_KG:R_KG + 1], ms_work[:],
                                               ALU.mult, ALU.mult).then_inc(headn_ready, 1)
                sine_part(1)
                q_tile(1)
                dve.wait_ge(rotc_ready, l + 1)
                dve.wait_ge(rots_ready, l * 5 + 2)
                for kv in range(N_KV_HEADS):
                    src = slice(kv * HEAD_DIM, (kv + 1) * HEAD_DIM)
                    for half in range(2):
                        ins = nc.vector.tensor_tensor(k_dup[half * HEAD_DIM:(half + 1) * HEAD_DIM, kv],
                                                      rot_c[src], rot_s[src], ALU.add)
                ins.then_inc(k_ready, 1)
                sine_part(2)
                split_lo(dve, l, 3)
                for j in (2, 3):
                    q_tile(j)
                    sine_part(j + 1)
                split_lo(dve, l, 4)
                scaled("u3", u_sb[:, 0, PAD:])
                for kv in range(2):
                    dve.wait_ge(evac[ps.slot(f"qn{kv}")], ps.before(f"qn{kv}", l) + 1)
                rot.link(nc.vector.reciprocal(q_scale[:], q_scale[:]))
                rot.close()

                def u_half(i):
                    (g, half), n = HALF_TILES[i], 1 + i // 2
                    h0 = half * HALF
                    if n >= 2 and half == 0:
                        dve.wait_ge(pooled_ready, l * 4 + (n - 1))
                    dve.wait_ge(filled[4], ps.before(side_name(i), l) + 1)
                    nc.vector.tensor_tensor(u_sb[:, n % 2, PAD + h0:PAD + h0 + HALF], side, rinv[:, h0:h0 + HALF],
                                            ALU.mult).then_inc(evac[4], 1)

                def pool_map_lo(n):
                    g = GROUPS[n]
                    s = ps.slot(f"pool{g}")
                    dve.wait_ge(mixhi_ready, mix_count(l, f"pool{g}"))
                    nc.vector.scalar_tensor_tensor(tok(mix_lo[:, 4 + g]), halves(s), par[:, R_PS + g:R_PS + g + 1],
                                                   tok(mix_hi[:, 4 + g].bitcast(f32)), ALU.mult, ALU.subtract)\
                      .then_inc(evac[s], 1)

                ch = Chain(dve, dve_attn, l, 5 * NB)

                def row_maxima(b):
                    nk, s, y = BLOCKS[b][1], ps.slot(f"scores{b}"), b % 2
                    dve.wait_ge(filled[s], ps.before(f"scores{b}", l) + 1)
                    view = slot[s][:, :, 0:2 * nk].rearrange("p a (t k) -> p a t k", t=2)
                    ch.link(nc.vector.tensor_reduce(nmax[:, y].rearrange("p (a t) -> p a t", a=2), view, op=ALU.max,
                                                    axis=AX.X, negate=True))
                    ch.link(nc.vector.tensor_tensor(nmax[:, y], nmax[:, y],
                                                    q_scale[:, b].rearrange("p j kv -> p (j kv)"), ALU.mult))
                    ch.link(nc.vector.tensor_tensor(nm[:, y], nmax[:, y], nsink[:], ALU.min))
                    nc.vector.tensor_tensor(sink_arg[:, y], nm[:, y], nsink[:], ALU.subtract).then_inc(nm_ready, 1)

                def divide(b):
                    nk, s, y = BLOCKS[b][1], ps.slot(f"scores{b}"), b % 2
                    dve.wait_ge(evac[s], ps.before(f"scores{b}", l) + 1)
                    ch.link(nc.vector.tensor_tensor(den[:, y], row_sum[:, y], sink_exp[:, y], ALU.add))
                    ch.link(nc.vector.reciprocal(rden[:, y], den[:, y]))
                    nc.vector.tensor_tensor(probs[:, y, :, 0:nk], probs[:, y, :, 0:nk],
                                            rden[:, y].unsqueeze(2).broadcast_to([P, 4, nk]), ALU.mult)\
                      .then_inc(probs_ready, 1)

                def meta_probs_out(b):
                    pt = ps.slot(f"probs_T{b}")
                    dve.wait_ge(filled[pt], ps.before(f"probs_T{b}", l) + 1)
                    nc.vector.tensor_copy(probs_meta[:, b % 2], slot[pt][0:N_META, 1, :]).then_inc(meta_out, 1)

                def heads_lo(b):
                    t0, nq = BLOCKS[b][0], CHUNK if b else N_META
                    hd = ps.slot(f"heads{b}")
                    dve.wait_ge(mixhi_ready, mix_count(l, f"heads{b}"))
                    src = slot[hd][:, 0, 0:4 * CHUNK].rearrange("p (t q) -> p t q", t=4)[:, :, 0:nq]
                    nc.vector.tensor_tensor(mix_lo[:, 0:4, t0:t0 + nq], src,
                                            mix_hi[:, 0:4, t0:t0 + nq].bitcast(f32), ALU.subtract)\
                      .then_inc(evac[hd], 1)

                for step in range(NB + 3):
                    if 3 <= step < NB + 2:
                        meta_probs_out(step - 2)
                    if step >= 3:
                        heads_lo(step - 3)
                    if step == NB:
                        pool_map_lo(1)
                        pooled_lo(2)
                        pooled_tile(3)
                    if 1 <= step <= NB:
                        divide(step - 1)
                    if step < NB:
                        row_maxima(step)
                    if step == MAP_AT[0]:
                        pool_map_lo(0)
                    if step == NB:
                        pooled_lo(3)
                        pool_map_lo(2)
                    if step == NB + 1:
                        split_lo(dve, l, U_OUT)
                    if side_done(step) is not None:
                        u_half(side_done(step))
                    if step in POOLED_AT[0:3]:
                        pooled_tile(POOLED_AT.index(step))
                    if step in POOL_LO_AT[0:2]:
                        pooled_lo(POOL_LO_AT.index(step))
                    if step == 4:
                        split_lo(dve, l, U_POOL)
                pool_map_lo(3)
                ch.close()
                split_lo(dve, l, U_OUT + 1)

                def add_to_h(name, k):
                    s = ps.slot(name)
                    dve.wait_ge(filled[s], ps.before(name, l) + 1)
                    nc.vector.tensor_tensor(tok(h[:, k]), halves(s), tok(h[:, k]), ALU.add).then_inc(evac[s], 1)

                for j in range(4):
                    for k in (2 * j, 2 * j + 1):
                        add_to_h(f"out{k}", k)
                    if j < 3:
                        split_lo(dve, l, U_OUT + 2 + j)
                    for k in (2 * j, 2 * j + 1):
                        gain_lo(k, l * (2 * KT) + (KT + k + 1), par[:, R_FG:R_FG + KT])
                split_lo(dve, l, U_OUT + 5)

                inverse_rms_ready("ffn_norm")
                for c in range(2):
                    nc.vector.memset(gate[c][:, 0:2], 0.0)
                taps = par[:, R_CW:R_CW + 4 * FT].rearrange("p (t f) -> p t f", t=4)
                with dve.Fori(0, FI) as i:
                    ch = Chain(dve, dve_ffn, l * FI + i, 3)
                    ch.link(nc.vector.tensor_copy(cpar[:], taps[:, :, bass.ds(i * 2, 2)]))
                    for c in range(2):
                        scaled(f"gate{c}", gate[c][:, 2:], i)
                    split_lo(dve, l, U_FFN + 2, i)
                    for c in range(2):
                        dve.wait_ge(tap2_ready, l * FT + i * 2 + (c + 1))
                        ch.link(nc.vector.scalar_tensor_tensor(conv[c][:], gate[c][:, 1:1 + L], cpar[:, 1, c:c + 1],
                                                               conv[c][:], ALU.mult, ALU.add))
                        nc.vector.scalar_tensor_tensor(conv[c][:], gate[c][:, 0:L], cpar[:, 0, c:c + 1],
                                                       conv[c][:], ALU.mult, ALU.add).then_inc(conv_ready, 1)
                    ch.close()
                    for c in range(2):
                        scaled(f"up{c}", up[c][:], i)
                    split_lo(dve, l, U_FFN + 3, i)
                    for c in range(2):
                        dve.wait_ge(mhi_ready, l * FT + i * 2 + (c + 1))
                        one = bass.ds(i * 2 + c, 1)
                        nc.vector.tensor_tensor(m_lo[:, one].rearrange("p a t -> p (a t)"), up[c][:],
                                                m_hi[:, one].rearrange("p a t -> p (a t)").bitcast(f32),
                                                ALU.subtract).then_inc(mlo_ready, 1)
                nc.vector.tensor_copy(gain_next[:], gains_all[:, bass.ds(l + 1, 1)].rearrange("p a k -> p (a k)"))\
                  .then_inc(gains_ready, 1)
                for j in range(4):
                    for n in range(3):
                        unit = U_DOWN + 3 * j + n
                        if n == 2:
                            for k in (2 * j, 2 * j + 1):
                                add_to_h(f"down{k}", k)
                        if unit + 2 < UNITS:
                            split_lo(dve, l, unit + 2)

            for t in range(SEQ // P):
                dve.wait_ge(filled[t], ps.PROLOGUE[t] + ps.uses[t] * DEPTH + 1)
                nc.vector.tensor_copy(y_out[:, t, 512:], slot[t][:, 1, :]).then_inc(y_ready[1], 1)


def constant_table():
    import numpy as np

    table = np.zeros((P, NCONST), np.float32)
    table[:, C_ID:C_ID + P] = np.eye(P, dtype=np.float32)
    heads = np.arange(P) // HEAD_DIM
    table[:, C_BLK:C_BLK + P] = (heads[:, None] == heads[None, :]).astype(np.float32) / HEAD_DIM
    table[:, C_ONE:C_ONE + P] = 1.0 / D_MODEL
    t = np.arange(PAD)
    for g, w in enumerate(POOL_SIZES):
        table[:, C_CNT + g * PAD:C_CNT + (g + 1) * PAD] = w / np.minimum(t + 1, w)
    half = HEAD_DIM // 2
    inv = (1.0 / (np.float32(ROPE_THETA) ** (np.arange(0, HEAD_DIM, 2, dtype=np.float32) / np.float32(HEAD_DIM))))
    angle = np.arange(L, dtype=np.float32)[None, :] * inv.astype(np.float32)[:, None]
    feature = np.arange(P) % half
    sign = np.where(np.arange(P) % HEAD_DIM < half, 1.0, -1.0).astype(np.float32)
    table[:, C_COS:C_COS + L] = np.cos(angle)[feature]
    table[:, C_SIN:C_SIN + L] = np.sin(angle)[feature] * sign[:, None]
    return table


_INS = ["x", "meta_tokens", "attn_norm_g", "w_in", "q_norm_g", "k_norm_g", "sinks", "w_pool", "pool_scale",
        "w_out", "ffn_norm_g", "w_gate", "w_up", "conv_w", "conv_b", "w_down"]


def kernel(**inputs):
    import numpy as _np
    import concourse.bacc as _bacc
    from concourse.bass_utils import run_bass_kernel_spmd as _run

    nc = _bacc.Bacc("TRN2", target_bir_lowering=False, num_devices=1, dynamic_dma_scratch_size=256)
    arrays, args = {}, []
    for name in _INS:
        a = _np.ascontiguousarray(inputs[name])
        arrays[f"in_{name}"] = a
        args.append(nc.dram_tensor(f"in_{name}", a.shape, mybir.dt.from_np(a.dtype), kind="ExternalInput").ap())
    table = constant_table()
    arrays["const_table"] = table
    args.append(nc.dram_tensor("const_table", table.shape, mybir.dt.float32, kind="ExternalInput").ap())
    args.append(nc.dram_tensor("out", (1, SEQ, D_MODEL), mybir.dt.float32, kind="ExternalOutput").ap())
    build_trunk(nc, *args)
    result = _run(nc, [arrays], core_ids=[0])
    return result.results[0]["out"]
```
